# Optimizing a Trainium2 kernel written in Bass

```python
import jax, jax.numpy as jnp
from jax import lax
import numpy as np

'''Hybrid decoder trunk: DEPTH layers, each = RMSNorm -> one combined input projection whose
columns are partitioned among three parallel head groups (RWKV-7 time mixing, multi-scale
retention in chunkwise form, chunked gated DeltaNet with short causal conv) -> concatenation
over head groups -> one output projection -> residual; then RMSNorm -> hierarchical MoE
(top-1 expert group, top-2 experts inside it) -> residual. Final RMSNorm.
Inputs: x (BATCH, SEQ, D_MODEL) float32, positions (BATCH, SEQ) int32, per-layer weights
stacked on a leading DEPTH axis. Output: (BATCH, SEQ, D_MODEL).'''

D_MODEL = 2048
BATCH = 1
SEQ = 256
DEPTH = 1

D_MIX = D_MODEL
RWKV_W = 3 * D_MIX // 8
RET_W = D_MIX // 4
GDN_W = D_MIX - RWKV_W - RET_W
RWKV_HEAD_DIM = 64
RET_HEAD_DIM = 128
GDN_HEAD_DIM = 128
RWKV_HEADS = RWKV_W // RWKV_HEAD_DIM
RET_HEADS = RET_W // RET_HEAD_DIM
GDN_HEADS = GDN_W // GDN_HEAD_DIM
RWKV_DECAY_RANK = 96
RWKV_A_RANK = 96
RWKV_VRES_RANK = 64
RWKV_DECAY_SCALE = 0.6065306597126334
RWKV_GN_EPS = 64e-5
RET_CHUNK = 128
RET_GN_EPS = 1e-5
ROPE_BASE = 10000.0
GDN_CONV = 4
GDN_CHUNK = 64
MOE_GROUPS = 4
MOE_EXPERTS_PER_GROUP = 8
MOE_EXPERTS = MOE_GROUPS * MOE_EXPERTS_PER_GROUP
MOE_TOP_K = 2
MOE_HIDDEN = D_MODEL // 8
NORM_EPS = 1e-6
IN_SPLITS = (RWKV_W,) * 4 + (RET_W,) * 4 + (GDN_W,) * 4 + (GDN_HEADS,) * 2
N_IN = sum(IN_SPLITS)

kernel_name = "hybrid_rwkv7_retnet_gdn_hmoe"

def _rms_norm(x, w, eps=NORM_EPS):
    xf = x.astype(jnp.float32)
    y = xf * lax.rsqrt(jnp.mean(xf * xf, axis=-1, keepdims=True) + eps)
    return (y * w.astype(jnp.float32)).astype(x.dtype)

def _token_shift(x):
    pad = [(0, 0)] * x.ndim
    pad[1] = (1, 0)
    return jnp.pad(x[:, :-1], pad)

def _split_heads(t, n_heads):
    return t.reshape(*t.shape[:-1], n_heads, t.shape[-1] // n_heads)

def _l2norm(t, eps=1e-6):
    return t * lax.rsqrt(jnp.sum(t * t, axis=-1, keepdims=True) + eps)

def _head_norm(t, eps):
    mu = jnp.mean(t, axis=-1, keepdims=True)
    var = jnp.mean(jnp.square(t - mu), axis=-1, keepdims=True)
    y = (t - mu) * lax.rsqrt(var + eps)
    return y.reshape(*t.shape[:-2], -1)

def _to_chunks(t, c):
    b, s = t.shape[:2]
    return t.reshape(b, s // c, c, *t.shape[2:]).swapaxes(2, 3)

def _from_chunks(t):
    t = t.swapaxes(2, 3)
    return t.reshape(t.shape[0], -1, *t.shape[3:])

def _rwkv7_recurrence(r, w, k, v, kk, a):
    b, s, h, n = r.shape

    def step(state, inp):
        r_t, w_t, k_t, v_t, kk_t, a_t = inp
        sa = jnp.einsum('bhvk,bhk->bhv', state, -kk_t)
        state = (state * w_t[:, :, None, :]
                 + sa[..., None] * (kk_t * a_t)[:, :, None, :]
                 + v_t[..., None] * k_t[:, :, None, :])
        return state, jnp.einsum('bhvk,bhk->bhv', state, r_t)

    xs = tuple(jnp.moveaxis(t, 1, 0) for t in (r, w, k, v, kk, a))
    _, o = lax.scan(step, jnp.zeros((b, h, n, n), jnp.float32), xs)
    return jnp.moveaxis(o, 0, 1)

def _rwkv7_mix(h, r, k, v, g, mu_rkvg, mu_wa, w0, w1, w2, a0, a1, a2, k_k, k_a, r_k,
               ln_w, ln_b, v_first, vres):
    f32 = jnp.float32
    p = jnp.stack([r, k, v, g], axis=2).astype(f32)
    p = p + (_token_shift(p) - p) * mu_rkvg
    r, k, v, g = p[:, :, 0], p[:, :, 1], p[:, :, 2], p[:, :, 3]
    hf = h.astype(f32)
    dh = _token_shift(hf) - hf
    xw = hf + dh * mu_wa[0]
    xa = hf + dh * mu_wa[1]
    log_w = -RWKV_DECAY_SCALE * jax.nn.sigmoid(w0 + jnp.tanh(xw @ w1) @ w2)
    a = jax.nn.sigmoid(a0 + (xa @ a1) @ a2)
    if vres is None:
        v_first = v
    else:
        mu_v, v0, v1, v2 = vres
        xv = hf + dh * mu_v
        v = v + (v_first - v) * jax.nn.sigmoid(v0 + (xv @ v1) @ v2)
    kk = _l2norm(_split_heads(k * k_k, RWKV_HEADS))
    k = k * (1.0 + (a - 1.0) * k_a)
    r_h, k_h, v_h, a_h, w_h = (_split_heads(t, RWKV_HEADS) for t in (r, k, v, a, jnp.exp(log_w)))
    o = _rwkv7_recurrence(r_h, w_h, k_h, v_h, kk, a_h)
    o = _head_norm(o, RWKV_GN_EPS) * ln_w + ln_b
    bonus = (jnp.sum(r_h * k_h * r_k, axis=-1, keepdims=True) * v_h).reshape(o.shape)
    return (o + bonus) * jax.nn.sigmoid(g), v_first

def _rotary(t, positions):
    d = t.shape[-1]
    inv_freq = ROPE_BASE ** (-jnp.arange(0, d, 2, dtype=jnp.float32) / d)
    ang = positions.astype(jnp.float32)[..., None] * inv_freq
    cos = jnp.cos(ang)[:, :, None, :]
    sin = jnp.sin(ang)[:, :, None, :]
    t1, t2 = t[..., : d // 2], t[..., d // 2:]
    return jnp.concatenate([t1 * cos - t2 * sin, t1 * sin + t2 * cos], axis=-1)

def _retention_chunked(q, k, v, log_gamma):
    c = RET_CHUNK
    b, _, h, dk = q.shape
    dv = v.shape[-1]
    q, k, v = (_to_chunks(t, c) for t in (q, k, v))
    idx = jnp.arange(c, dtype=jnp.float32)
    diff = idx[:, None] - idx[None, :]
    dmask = jnp.where(diff >= 0, jnp.exp(jnp.maximum(diff, 0.0) * log_gamma[:, None, None]), 0.0)
    scores = jnp.einsum('bnhid,bnhjd->bnhij', q, k) * dmask
    inner = jnp.einsum('bnhij,bnhjv->bnhiv', scores, v)
    kdec = k * jnp.exp((c - 1 - idx) * log_gamma[:, None])[:, :, None]
    kv = jnp.einsum('bnhjk,bnhjv->bnhkv', kdec, v)
    chunk_decay = jnp.exp(c * log_gamma)[:, None, None]

    def step(state, kv_n):
        return state * chunk_decay + kv_n, state

    _, r_prev = lax.scan(step, jnp.zeros((b, h, dk, dv), jnp.float32), jnp.moveaxis(kv, 1, 0))
    r_prev = jnp.moveaxis(r_prev, 0, 1)
    qdec = q * jnp.exp((idx + 1.0) * log_gamma[:, None])[:, :, None]
    cross = jnp.einsum('bnhik,bnhkv->bnhiv', qdec, r_prev)
    return _from_chunks(inner + cross)

def _retnet_mix(q, k, v, g, positions, gn_w):
    f32 = jnp.float32
    q = _rotary(_split_heads(q.astype(f32), RET_HEADS), positions)
    k = _rotary(_split_heads(k.astype(f32), RET_HEADS), positions) * RET_HEAD_DIM ** -0.5
    v = _split_heads(v.astype(f32), RET_HEADS)
    log_gamma = jnp.log(1.0 - 2.0 ** (-5.0 - jnp.arange(RET_HEADS, dtype=f32)))
    y = _retention_chunked(q, k, v, log_gamma)
    y = _head_norm(y, RET_GN_EPS) * gn_w
    return jax.nn.silu(g.astype(f32)) * y

def _causal_depthwise_conv(x, w):
    kw, c = w.shape
    return lax.conv_general_dilated(x, w[:, None, :].astype(x.dtype), window_strides=(1,),
                                    padding=[(kw - 1, 0)], dimension_numbers=('NWC', 'WIO', 'NWC'),
                                    feature_group_count=c)

def _gated_delta_chunked(q, k, v, g, beta):
    c = GDN_CHUNK
    q, k, v, g, beta = (_to_chunks(t, c) for t in (q, k, v, g, beta))
    b, _, h, _, dk = q.shape
    dv = v.shape[-1]
    gc = jnp.cumsum(g, axis=-1)
    causal = jnp.tril(jnp.ones((c, c), bool))
    strict = jnp.tril(jnp.ones((c, c), bool), -1)
    decay = jnp.exp(jnp.where(causal, gc[..., :, None] - gc[..., None, :], -jnp.inf))
    kb = k * beta[..., None]
    lower = jnp.where(strict, jnp.einsum('bnhid,bnhjd->bnhij', kb, k) * decay, 0.0)
    rhs = jnp.concatenate([v * beta[..., None], kb * jnp.exp(gc)[..., None]], axis=-1)
    sol = lax.linalg.triangular_solve(lower + jnp.eye(c, dtype=lower.dtype), rhs,
                                      left_side=True, lower=True, unit_diagonal=True)
    u, w = sol[..., :dv], sol[..., dv:]
    attn = jnp.einsum('bnhid,bnhjd->bnhij', q, k) * decay
    g_last = gc[..., -1]
    qg = q * jnp.exp(gc)[..., None]
    kd = k * jnp.exp(g_last[..., None] - gc)[..., None]

    def step(state, inp):
        qg_n, kd_n, u_n, w_n, attn_n, gl_n = inp
        v_new = u_n - jnp.einsum('bhck,bhkv->bhcv', w_n, state)
        o = jnp.einsum('bhck,bhkv->bhcv', qg_n, state) + jnp.einsum('bhij,bhjv->bhiv', attn_n, v_new)
        state = state * jnp.exp(gl_n)[..., None, None] + jnp.einsum('bhck,bhcv->bhkv', kd_n, v_new)
        return state, o

    xs = tuple(jnp.moveaxis(t, 1, 0) for t in (qg, kd, u, w, attn, g_last))
    _, o = lax.scan(step, jnp.zeros((b, h, dk, dv), jnp.float32), xs)
    return _from_chunks(jnp.moveaxis(o, 0, 1))

def _gdn_mix(q, k, v, z, a, b, conv_w, a_log, dt_bias, norm_w):
    f32 = jnp.float32
    qkv = jnp.concatenate([q, k, v], axis=-1).astype(f32)
    qkv = jax.nn.silu(_causal_depthwise_conv(qkv, conv_w.astype(f32)))
    q, k, v = jnp.split(qkv, 3, axis=-1)
    q = _l2norm(_split_heads(q, GDN_HEADS)) * GDN_HEAD_DIM ** -0.5
    k = _l2norm(_split_heads(k, GDN_HEADS))
    v = _split_heads(v, GDN_HEADS)
    beta = jax.nn.sigmoid(b.astype(f32))
    g = -jnp.exp(a_log.astype(f32)) * jax.nn.softplus(a.astype(f32) + dt_bias)
    o = _gated_delta_chunked(q, k, v, g, beta)
    o = (o * lax.rsqrt(jnp.mean(o * o, axis=-1, keepdims=True) + NORM_EPS)).reshape(*o.shape[:-2], -1)
    return o * norm_w * jax.nn.silu(z.astype(f32))

def _hier_moe(x, group_w, group_b, expert_w, expert_b, w1, w3, w2):
    f32 = jnp.float32
    b, s, d = x.shape
    xt = x.reshape(b * s, d)
    group_logits = (xt @ group_w + group_b).astype(f32)
    group_probs = jax.nn.softmax(group_logits, axis=-1)
    group_idx = jnp.argmax(group_logits, axis=-1)
    group_gate = jnp.take_along_axis(group_probs, group_idx[:, None], axis=-1)
    expert_logits = (xt @ expert_w + expert_b).astype(f32).reshape(-1, MOE_GROUPS, MOE_EXPERTS_PER_GROUP)
    in_group = jnp.take_along_axis(expert_logits, group_idx[:, None, None], axis=1)[:, 0]
    top_p, top_i = lax.top_k(jax.nn.softmax(in_group, axis=-1), MOE_TOP_K)
    top_p = top_p / jnp.sum(top_p, axis=-1, keepdims=True)
    within = jnp.sum(top_p[..., None] * jax.nn.one_hot(top_i, MOE_EXPERTS_PER_GROUP, dtype=f32), axis=-2)
    gates = (group_gate * jax.nn.one_hot(group_idx, MOE_GROUPS, dtype=f32))[:, :, None] * within[:, None, :]
    gates = gates.reshape(-1, MOE_EXPERTS).astype(x.dtype)
    hid = jax.nn.silu(jnp.einsum('td,edf->tef', xt, w1)) * jnp.einsum('td,edf->tef', xt, w3)
    y = jnp.einsum('tef,efd->td', hid * gates[..., None], w2)
    return y.reshape(b, s, d)

def setup_inputs(seed: int = 0) -> dict:
    key = jax.random.key(seed)
    keys = iter(jax.random.split(key, 40))
    f32 = jnp.float32

    def nrm(shape, scale):
        return scale * jax.random.normal(next(keys), shape, f32)

    def uni(shape, lo, hi):
        return jax.random.uniform(next(keys), shape, f32, lo, hi)

    L, Lv, D = DEPTH, DEPTH - 1, D_MODEL
    x = nrm((BATCH, SEQ, D), 1.0)
    offset = jax.random.randint(next(keys), (BATCH, 1), 0, 4096, dtype=jnp.int32)
    positions = (offset + jnp.arange(SEQ, dtype=jnp.int32)[None, :]).astype(jnp.int32)
    dt = jnp.exp(uni((L, GDN_HEADS), float(np.log(1e-3)), float(np.log(1e-1))))
    gdn_dt_bias = dt + jnp.log(-jnp.expm1(-dt))
    gdn_a_log = jnp.log(uni((L, GDN_HEADS), 1.0, 16.0))
    return {
        'x': x,
        'positions': positions,
        'norm1_w': 1.0 + nrm((L, D), 0.02),
        'w_in': nrm((L, D, N_IN), D ** -0.5),
        'w_out': nrm((L, D_MIX, D), D_MIX ** -0.5),
        'rwkv_mu_rkvg': uni((L, 4, RWKV_W), 0.0, 1.0),
        'rwkv_mu_wa': uni((L, 2, D), 0.0, 1.0),
        'rwkv_w0': uni((L, RWKV_W), -2.0, 2.0),
        'rwkv_w1': nrm((L, D, RWKV_DECAY_RANK), D ** -0.5),
        'rwkv_w2': nrm((L, RWKV_DECAY_RANK, RWKV_W), 0.5 * RWKV_DECAY_RANK ** -0.5),
        'rwkv_a0': nrm((L, RWKV_W), 0.5),
        'rwkv_a1': nrm((L, D, RWKV_A_RANK), D ** -0.5),
        'rwkv_a2': nrm((L, RWKV_A_RANK, RWKV_W), 0.5 * RWKV_A_RANK ** -0.5),
        'rwkv_k_k': uni((L, RWKV_W), 0.7, 1.0),
        'rwkv_k_a': uni((L, RWKV_W), 0.8, 1.2),
        'rwkv_r_k': nrm((L, RWKV_HEADS, RWKV_HEAD_DIM), 0.1),
        'rwkv_ln_w': 1.0 + nrm((L, RWKV_W), 0.02),
        'rwkv_ln_b': nrm((L, RWKV_W), 0.02),
        'rwkv_mu_vres': uni((Lv, D), 0.0, 1.0),
        'rwkv_v0': nrm((Lv, RWKV_W), 0.5),
        'rwkv_v1': nrm((Lv, D, RWKV_VRES_RANK), D ** -0.5),
        'rwkv_v2': nrm((Lv, RWKV_VRES_RANK, RWKV_W), 0.5 * RWKV_VRES_RANK ** -0.5),
        'ret_gn_w': 1.0 + nrm((L, RET_W), 0.02),
        'gdn_conv_w': nrm((L, GDN_CONV, 3 * GDN_W), GDN_CONV ** -0.5),
        'gdn_a_log': gdn_a_log,
        'gdn_dt_bias': gdn_dt_bias,
        'gdn_norm_w': 1.0 + nrm((L, GDN_W), 0.02),
        'norm2_w': 1.0 + nrm((L, D), 0.02),
        'moe_group_w': nrm((L, D, MOE_GROUPS), D ** -0.5),
        'moe_group_b': nrm((L, MOE_GROUPS), 0.01),
        'moe_expert_w': nrm((L, D, MOE_EXPERTS), D ** -0.5),
        'moe_expert_b': nrm((L, MOE_EXPERTS), 0.01),
        'moe_w1': nrm((L, MOE_EXPERTS, D, MOE_HIDDEN), D ** -0.5),
        'moe_w3': nrm((L, MOE_EXPERTS, D, MOE_HIDDEN), D ** -0.5),
        'moe_w2': nrm((L, MOE_EXPERTS, MOE_HIDDEN, D), MOE_HIDDEN ** -0.5),
        'final_norm_w': 1.0 + nrm((D,), 0.02),
    }

def reference(x, positions, norm1_w, w_in, w_out,
              rwkv_mu_rkvg, rwkv_mu_wa, rwkv_w0, rwkv_w1, rwkv_w2, rwkv_a0, rwkv_a1, rwkv_a2,
              rwkv_k_k, rwkv_k_a, rwkv_r_k, rwkv_ln_w, rwkv_ln_b,
              rwkv_mu_vres, rwkv_v0, rwkv_v1, rwkv_v2,
              ret_gn_w, gdn_conv_w, gdn_a_log, gdn_dt_bias, gdn_norm_w,
              norm2_w, moe_group_w, moe_group_b, moe_expert_w, moe_expert_b,
              moe_w1, moe_w3, moe_w2, final_norm_w):
    split_points = np.cumsum(IN_SPLITS)[:-1].tolist()
    v_first = None
    for l in range(DEPTH):
        h = _rms_norm(x, norm1_w[l])
        (rr, rk, rv, rg, tq, tk, tv, tg, dq, dk, dv, dz, da, db) = jnp.split(h @ w_in[l], split_points, axis=-1)
        vres = None if l == 0 else (rwkv_mu_vres[l - 1], rwkv_v0[l - 1], rwkv_v1[l - 1], rwkv_v2[l - 1])
        out_a, v_first = _rwkv7_mix(h, rr, rk, rv, rg, rwkv_mu_rkvg[l], rwkv_mu_wa[l], rwkv_w0[l],
                                    rwkv_w1[l], rwkv_w2[l], rwkv_a0[l], rwkv_a1[l], rwkv_a2[l],
                                    rwkv_k_k[l], rwkv_k_a[l], rwkv_r_k[l], rwkv_ln_w[l], rwkv_ln_b[l],
                                    v_first, vres)
        out_b = _retnet_mix(tq, tk, tv, tg, positions, ret_gn_w[l])
        out_c = _gdn_mix(dq, dk, dv, dz, da, db, gdn_conv_w[l], gdn_a_log[l], gdn_dt_bias[l], gdn_norm_w[l])
        mixed = jnp.concatenate([out_a, out_b, out_c], axis=-1).astype(x.dtype)
        x = x + mixed @ w_out[l]
        x = x + _hier_moe(_rms_norm(x, norm2_w[l]), moe_group_w[l], moe_group_b[l], moe_expert_w[l],
                          moe_expert_b[l], moe_w1[l], moe_w3[l], moe_w2[l])
    return _rms_norm(x, final_norm_w)


_drawn_inputs = setup_inputs


def setup_inputs(seed=0):
    import zlib

    import numpy as np

    out = dict(_drawn_inputs(seed))
    spreads = {}
    factors = {'rwkv_k_k': 3.937,
     'rwkv_ln_w': 16.365,
     'rwkv_ln_b': 13.287,
     'ret_gn_w': 16.22,
     'gdn_norm_w': 12.918,
     'moe_group_b': 13.084,
     'moe_expert_b': 23.25,
     'final_norm_w': 8.415,
     'norm2_w': 4.467}
    for name, (base, spread) in spreads.items():
        noise = np.random.default_rng([zlib.crc32(name.encode()), seed]).standard_normal(out[name].shape)
        drawn = base * np.exp(spread * noise) if base else spread * noise
        out[name] = __import__('jax').numpy.asarray(drawn.astype(out[name].dtype))
    for name, factor in factors.items():
        out[name] = (out[name] * factor).astype(out[name].dtype)
    return out
```

```python
from contextlib import ExitStack

import numpy as np

import concourse.bass as bass
from concourse import mybir

F32 = mybir.dt.float32
I32 = mybir.dt.int32
ALU = mybir.AluOpType
ACT = mybir.ActivationFunctionType
AX = mybir.AxisListType.X

P = 128
D = 2048
T = 256
TT = T // P
K = D // P
RW, RT, GD = 768, 512, 768
NJ = RW // P
NH = GD // P
RH = RT // P
N_IN = 4 * RW + 4 * RT + 4 * GD + 2 * NH
CH = 64
NC = T // CH
DECAY = 0.6065306597126334
NE, TOPC, HID = 32, 32, 256
PASSES = T // TOPC
CW = 256
NTOK = 3 * RT // CW
COL_RWKV, COL_RET, COL_RETG, COL_GDN, COL_AB = 0, 4 * RW, 4 * RW + 3 * RT, 4 * RW + 4 * RT, N_IN - 2 * NH
PI_LO = 3.1415925
LEVELS = 6


SEGMENTS = [(24, COL_GDN), (30, COL_GDN + GD), (36, COL_GDN + 2 * GD), (0, COL_RWKV), (6, COL_RWKV + RW),
            (12, COL_RWKV + 2 * RW), (42, COL_GDN + 3 * GD), (18, COL_RWKV + 3 * RW), (48, COL_RETG)]
NCHUNK = NTOK + 26


def param_columns():
    at, col = 0, {}
    for name, n in (("mu", 4 * NJ), ("w0", NJ), ("a0", NJ), ("k_k", NJ), ("k_a", NJ), ("r_k", NJ), ("ln_w", NJ),
                    ("ln_b", NJ), ("gn_w", RH), ("gdn_w", NH), ("conv", 4 * 3 * NH), ("norm1", K), ("mu_w", K),
                    ("mu_a", K), ("norm2", K), ("dt", NH), ("alog", NH), ("router_b", 36)):
        col[name] = at
        at += n
    return col, at


def const_arrays():
    s, t = np.arange(P)[:, None], np.arange(P)[None, :]
    same = (s // CH) == (t // CH)
    lg = np.log(1.0 - 2.0 ** (-5.0 - np.arange(RH)))
    out = {"ident": s == t,
           "stack": (s % TOPC) == np.arange(TOPC)[None, :],
           "iota": np.broadcast_to(np.arange(NE)[None, :], (P, NE)),
           "bd": same,
           "incl": same & (s <= t),
           "strict": same & (s < t),
           "after": same & (s > t),
           "ones": np.ones((P, P)),
           "before": s < t}
    for lv in range(LEVELS):
        b = 2 ** lv
        out[f"lev{lv}"] = ((s // b) % 2 == 0) & (t // b == s // b + 1)
    out["carry"] = np.broadcast_to(np.arange(T)[None, :] % CH != 0, (P, T))
    out["dmask"] = np.concatenate([np.where(s <= t, np.exp(np.maximum(t - s, 0) * g), 0.0) for g in lg], 1) * P ** -0.5
    out["qdec"] = np.exp((s + 1.0) * lg[None, :])
    out["kdec"] = np.exp((P - 1.0 - s) * lg[None, :]) * P ** -0.5
    out["freq"] = np.broadcast_to((np.float32(10000.0) ** (-np.arange(0, P, 2, dtype=np.float32) / P))[None, :], (P, 64))
    return {n: np.ascontiguousarray(a, dtype=np.float32) for n, a in out.items()}


def trunk(nc, x, positions, w_in, w_out, lora1, lora2, par, consts, router, w1, w3, w2, final_w, xt_dram, out):
    col, npar = param_columns()
    ccol, at = {}, 0
    for name, a in const_arrays().items():
        ccol[name] = (at, a.shape[1])
        at += a.shape[1]
    ncon = at

    with ExitStack() as ctx:
        def sem(name):
            return ctx.enter_context(nc.semaphore(name))

        mem = ctx.enter_context(nc.sbuf_tensor("mem", [P, 204 * 256], F32))
        prm = ctx.enter_context(nc.sbuf_tensor("prm", [P, npar], F32))
        small = ctx.enter_context(nc.sbuf_tensor("small", [P, 320], F32))
        posi = ctx.enter_context(nc.sbuf_tensor("posi", [P, TT], I32))
        flag = ctx.enter_context(nc.sbuf_tensor("flag", [P, 1], I32))
        bank = [ctx.enter_context(nc.psum_tensor(f"bank{i}", [P, 512], F32)) for i in range(8)]

        def view(kb, *shape):
            n = int(np.prod(shape))
            assert kb * 256 + n <= 204 * 256
            v = mem[:, int(kb * 256):int(kb * 256) + n]
            if len(shape) == 2:
                v = v.rearrange("p (a b) -> p a b", a=shape[0])
            elif len(shape) == 3:
                v = v.rearrange("p (a b c) -> p a b c", a=shape[0], b=shape[1])
            return v

        def con(name):
            a, n = ccol[name]
            return view(187, ncon)[:, a:a + n]

        def pcol(name, j, n=1):
            return prm[:, col[name] + j:col[name] + j + n]

        def over(ap, n):
            return ap.unsqueeze(1).broadcast_to([P, n, ap.shape[-1]])

        def tok(v):
            return v.rearrange("p a b -> p (a b)").rearrange("p (a c) -> p a c", a=TT)

        def wide(ap, n):
            return ap.unsqueeze(2).broadcast_to([P, ap.shape[-1], n])

        X = view(0, TT, D)
        PJ = view(16, 52, T)
        pr, pk, pv, pg = (PJ[:, NJ * i:NJ * i + NJ, :] for i in range(4))
        gq, gk, gv, gz = (PJ[:, 24 + NH * i:24 + NH * i + NH, :] for i in range(4))
        rg = PJ[:, 48:52, :]
        XW, XA, XN = view(16, K, T), view(32, K, T), view(48, TT, D)
        DH = view(48, K, T)
        TM = view(68, TT, 3 * RT)
        AB = small[:, 0:24].rearrange("p (a b) -> p a b", a=TT)
        HT = view(81, K, T)
        RING = [view(97 + 16 * b, K, CW) for b in range(3)]
        T1, T2, T3, T4, T5, T6, T7 = (view(145 + 6 * i, NJ, T) for i in range(7))
        L1 = view(145, 2, K, 96)
        L2 = view(169, 2, RW)
        WAB = view(200, K, 12)
        LH = view(201, 2, T)
        COS, SIN, ANG, ANR = (view(v, TT, 64) for v in (10, 10.5, 11, 11.5))
        QR, KR = view(175, TT, RT), view(181, TT, RT)
        QT, KT = view(0, TT, RH, P), view(12, TT, RH, P)
        KD0 = view(4, RT)
        ST = view(181, TT, RH, P)
        KV0 = view(175, RT)
        RTMP = view(198, RT)
        YR = view(6, TT * RH, P)
        YQ = view(198, 2 * RH, P)
        LT3, TM3, TI3, AS3, LK3 = (view(81 + 6 * i, 3, 512) for i in range(5))
        RB, RK = view(111, 6, 512), view(123, 6, 512)
        LM3 = view(135, 3, 512)
        EG, DT, LG = view(68, NH, T), view(74, NH * TT, P), view(198, NH * TT, P)
        KDG, VBG, WTG = view(68, TT, GD), view(0, TT, GD), view(10, NH, T)
        GTMP1, GTMP2 = view(175, 12, P), view(181, 12, P)
        CACC, CSQ = T1, T2
        X1 = view(99, 3, 256)
        M1, S1, MTMP = view(81, NJ, P), view(84, NH, P), view(87, NJ, P)
        OG = view(105, TT, GD)
        NTMP = view(87, TT * GD)
        MIX = view(111, K, T)
        WO = [view(v, D) for v in (127, 135, 145, 153, 169, 177)]
        XTT = view(16, K, T)
        XT = view(16, K, NE * TOPC)
        XS = view(129, TT, D)
        RWT = view(161, K, 36)
        PS, PG = view(145, TT, NE * TOPC), view(153, TT, NE * TOPC)
        WU = [view(81 + 48 * b, 2, K, HID) for b in range(2)]
        WD = [view(81 + 48 * b + 32, 2, D) for b in range(2)]
        SG = view(177, 8, T)
        YS, XE = view(188, D), [view(196 + 2 * b, K, TOPC) for b in range(2)]
        UP = [view(200 + 2 * b, 512) for b in range(2)]
        GS = view(185, 64)
        HD = [view(185.25 + 0.25 * b, 2, TOPC) for b in range(2)]
        SGQ = view(185.75, T)
        FW = view(81, D)
        JUNK = view(89, D)

        tiny = iter(range(24, 320))

        def cols(n):
            a = [next(tiny) for _ in range(n)]
            return small[:, a[0]:a[0] + n]

        ssq, rstd = cols(2), cols(2)
        elast = cols(24).rearrange("p (a b) -> p a b", a=NJ)
        glast = cols(24).rearrange("p (a b) -> p a b", a=NH)
        beta, gate, egc, ekd = cols(12), cols(12), cols(12), cols(12)
        gcum = cols(12)
        posf, stat, stat2 = cols(2), cols(24), cols(24)
        ea, eps6 = cols(6), cols(1)
        posm = cols(64).rearrange("p (a b) -> p a b", a=TT)
        LGT = view(163.5, TT, 36)
        GEX = view(164, TT, NE)
        R1, R2, R3, R4, R5, R6 = (view(164.5 + 0.25 * i, TT, NE) for i in range(6))
        GE = view(186.75, TT, NE)

        x_in, c_in, lora_in, ab_in = sem("x_in"), sem("c_in"), sem("lora_in"), sem("ab_in")
        win_in = [sem(f"win_in{b}") for b in range(3)]
        win_mm, win_out = sem("win_mm"), sem("win_out")
        dve, act = sem("dve"), sem("act")
        ss_ok, std_ok = sem("ss_ok"), sem("std_ok")
        ss_mm = sem("ss_mm")
        xn_ok, xt_mm, ht_ok = sem("xn_ok"), sem("xt_mm"), sem("ht_ok")
        xwa_ok, lo_mm, lo_ok, lo2_mm, sig_ok = sem("xwa_ok"), sem("lo_mm"), sem("lo_ok"), sem("lo2_mm"), sem("sig_ok")
        ang_ok, sin_ok, ab_mm, ab_ok = sem("ang_ok"), sem("sin_ok"), sem("ab_mm"), sem("ab_ok")
        rot_ok, rt_mm, rt_ok, ry_ok = sem("rot_ok"), sem("rt_mm"), sem("rt_ok"), sem("ry_ok")
        cum_ok, exp_ok, sq_ok, sq_mm = sem("cum_ok"), sem("exp_ok"), sem("sq_ok"), sem("sq_mm")
        bon_ok, bon_mm, bon_done, chan_ok = sem("bon_ok"), sem("bon_mm"), sem("bon_done"), sem("chan_ok")
        tok_mm, tok_ok = sem("tok_mm"), sem("tok_ok")
        conv_ok, silu_ok, gn_ok = sem("conv_ok"), sem("silu_ok"), sem("gn_ok")
        ga_ok, gb_ok, gate_ok, gate_mm, gexp_in, gexp_ok = (sem(n) for n in (
            "ga_ok", "gb_ok", "gate_ok", "gate_mm", "gexp_in", "gexp_ok"))
        prod_mm, prod_ok = sem("prod_mm"), sem("prod_ok")
        t0_ok, t0_mm, t0_sb = sem("t0_ok"), sem("t0_mm"), sem("t0_sb")
        lm_ok, a_mm, a_sb, t_mm, t_ok = sem("lm_ok"), sem("a_mm"), sem("a_sb"), sem("t_mm"), sem("t_ok")
        u1_mm, u1_ok, u2_mm, u2_ok = sem("u1_mm"), sem("u1_ok"), sem("u2_mm"), sem("u2_ok")
        m_ok, su_mm, su_ok, sm_mm, so_mm, so_ok = (sem(n) for n in ("m_ok", "su_mm", "su_ok", "sm_mm", "so_mm", "so_ok"))
        o_ok, mt_mm, mt_ok = sem("o_ok"), sem("mt_mm"), sem("mt_ok")
        x2_in, wo_mm = sem("x2_in"), sem("wo_mm")
        wo_in = [sem(f"wo_in{b}") for b in range(6)]
        x1_ok, xs_ok, xs_mm, xs_t, rw_in, lg_mm, rex_in, rex_ok = (sem(n) for n in (
            "x1_ok", "xs_ok", "xs_mm", "xs_t", "rw_in", "lg_mm", "rex_in", "rex_ok"))
        e_ok, pos_mm, flag_ok, xs_out, xs_in = sem("e_ok"), sem("pos_mm"), sem("flag_ok"), sem("xs_out"), sem("xs_in")
        p_ok, sg_mm, sg_ok, g_mm, g_act, g_dve = (sem(n) for n in ("p_ok", "sg_mm", "sg_ok", "g_mm", "g_act", "g_dve"))
        wu_in = [sem(f"wu_in{b}") for b in range(2)]
        wd_in = [sem(f"wd_in{b}") for b in range(2)]
        xe_ok, up_mm, up_sb, h_mm, gs_ok, hd_ok, dn_mm = (sem(n) for n in (
            "xe_ok", "up_mm", "up_sb", "h_mm", "gs_ok", "hd_ok", "dn_mm"))
        ya_ok, yd_ok, sc_mm, sc_ok, sq_stage = (sem(n) for n in ("ya_ok", "yd_ok", "sc_mm", "sc_ok", "sq_stage"))
        wu_free = [sem(f"wu_free{b}") for b in range(2)]
        wd_free = [sem(f"wd_free{b}") for b in range(2)]
        tok_a, tok_d, rt_dve, sx_mm, pass_go, fin_go, sgq_ok = (sem(n) for n in (
            "tok_a", "tok_d", "rt_dve", "sx_mm", "pass_go", "fin_go", "sgq_ok"))
        conv_in, gs_root, gates_ok, ya_half, yd_half, p_step, xs_stored = (sem(n) for n in (
            "conv_in", "gs_root", "gates_ok", "ya_half", "yd_half", "p_step", "xs_stored"))
        fw_in, fin_ss, fin_std, y_ok, out_done = (sem(n) for n in ("fw_in", "fin_ss", "fin_std", "y_ok", "out_done"))

        wv = w_in.rearrange("(p k) n -> p k n", k=K)
        w1v = w1.rearrange("e (p k) f -> p e (k f)", k=K)
        w3v = w3.rearrange("e (p k) f -> p e (k f)", k=K)
        w2v = w2.rearrange("e (f p) n -> p e f n", p=P)
        xv = x.rearrange("(a p) n -> p a n", p=P)
        ov = out.rearrange("(a p) n -> p a n", p=P)
        xdv = xt_dram.rearrange("(a p) n -> p a n", p=P)
        wov = w_out.rearrange("(k p) n -> p k n", p=P)

        block = ctx.enter_context(nc.Block())

        @block.sync
        def _(sp):
            sp.dma_start(X, xv).then_inc(x_in, 16)
            sp.dma_start(view(187, ncon), consts).then_inc(c_in, 16)
            sp.dma_start(prm[:], par).then_inc(c_in, 16)
            sp.dma_start(posi[:], positions).then_inc(c_in, 16)

            def load(n, b, c0):
                sp.dma_start(RING[b], wv[:, :, c0]).then_inc(win_in[b], 16)

            for n in range(NTOK):
                if n >= 3:
                    sp.wait_ge(win_mm, n - 2)
                load(n, n % 3, slice(COL_RET + n * CW, COL_RET + (n + 1) * CW))
                if n == 2:
                    sp.dma_start(WAB, wv[:, :, COL_AB:N_IN]).then_inc(ab_in, 16)
                    sp.dma_start(L1, lora1.rearrange("a (p k) r -> p a k r", k=K)).then_inc(lora_in, 16)
                    sp.dma_start(L2[0:96], lora2).then_inc(lora_in, 16)
            for first, c_from in ((NTOK, COL_GDN), (NTOK + 9, COL_RWKV)):
                with sp.Fori(0, 3) as i:
                    for b in range(3):
                        sp.wait_ge(win_mm, i * 3 + (first + b - 2))
                        load(None, b, bass.ds(i * (3 * CW) + (c_from + b * CW), CW))
            for n in range(NTOK + 18, NCHUNK):
                c0 = SEGMENTS[(n - NTOK) // 3][1] + (n - NTOK) % 3 * CW
                sp.wait_ge(win_mm, n - 2)
                load(n, n % 3, slice(c0, c0 + CW))
            sp.wait_ge(so_mm, TT)
            for k in range(K):
                if k >= 6:
                    sp.wait_ge(wo_mm, k - 5)
                sp.dma_start(WO[k % 6], wov[:, k, :]).then_inc(wo_in[k % 6], 16)
                if k == 5:
                    sp.wait_ge(mt_mm, 3)
                    sp.dma_start(X, xv).then_inc(x2_in, 16)
            sp.wait_ge(wo_mm, K)
            sp.dma_start(RWT, router.rearrange("(p k) n -> p k n", k=K)).then_inc(rw_in, 16)

            def experts(r):
                with sp.Fori(0, 8) as i:
                    for b in range(4):
                        s, e = b % 2, i * 4 + b
                        use = r * 17 + i * 2 + (b // 2 + 1)
                        sp.wait_ge(wu_free[s], use)
                        sp.dma_start(WU[s][:, 0].rearrange("p k f -> p (k f)").unsqueeze(1),
                                     w1v[:, bass.ds(e, 1), :]).then_inc(wu_in[s], 16)
                        sp.dma_start(WU[s][:, 1].rearrange("p k f -> p (k f)").unsqueeze(1),
                                     w3v[:, bass.ds(e, 1), :]).then_inc(wu_in[s], 16)
                        sp.wait_ge(wd_free[s], use)
                        sp.dma_start(WD[s].unsqueeze(1), w2v[:, bass.ds(e, 1), :, :]).then_inc(wd_in[s], 16)

            experts(0)
            sp.wait_ge(flag_ok, 1)
            with sp.If(sp.value_load(flag[0:1, 0:1]) == 1):
                sp.wait_ge(xs_stored, 1)
                with sp.Fori(1, PASSES) as r:
                    sp.wait_ge(pass_go, r)
                    sp.dma_start(XS, xdv).then_inc(xs_in, 16)
                    experts(r)
            sp.wait_ge(fin_go, 1)
            sp.dma_start(FW, final_w).then_inc(fw_in, 16)
            for a in range(TT):
                sp.wait_ge(y_ok, a + 1)
                sp.dma_start(ov[:, a], X[:, a]).then_inc(out_done, 16)
            sp.wait_ge(out_done, 16 * TT)

        @block.gpsimd
        def _(pool):
            for bt in range(3):
                for lv in range(1, LEVELS):
                    n = (bt * (LEVELS - 1) + lv - 1) * 3
                    for g in range(3):
                        pool.wait_ge(prod_ok, 7 + bt * 12 + g * 4 if bt < 2 else 6)
                        if n:
                            pool.wait_ge(a_mm, n - 3 + g + 1)
                        src = LT3[:, g, :].rearrange("p (q c) -> p q c", q=4) if bt < 2 else LG[:, 4 * g:4 * g + 4, :]
                        nc.gpsimd.tensor_tensor(LM3[:, g, :].rearrange("p (q c) -> p q c", q=4), src,
                                                over(con(f"lev{lv}"), 4), ALU.mult).then_inc(lm_ok, 1)
            pool.wait_ge(xs_ok, 1)
            pool.dma_start(xdv, XS).then_inc(xs_out, 16)
            pool.wait_ge(xs_out, 16)
            pool.sem_inc(xs_stored, 1)

        @block.tensor
        def _(pe):
            mm = nc.tensor.matmul
            ident, stack = con("ident"), con("stack")

            pe.wait_ge(c_in, 48)
            pe.wait_ge(xn_ok, 1)
            xn = XN.rearrange("p a (d k) -> p a k d", k=K)
            for r in range(8):
                if r >= 4:
                    pe.wait_ge(ht_ok, r - 3)
                for kk in range(2):
                    for a in range(TT):
                        o = kk * T + a * P
                        last = nc.tensor.transpose(bank[3 + r % 4][:, o:o + P], xn[:, a, 2 * r + kk, :], ident)
                last.then_inc(xt_mm, 1)
            pe.wait_ge(ht_ok, 8)

            def win_token(b):
                for a in range(TT):
                    for k in range(K):
                        last = mm(bank[b][:, a * CW:(a + 1) * CW], HT[:, k, a * P:(a + 1) * P], RING[b][:, k, :],
                                  start=(k == 0), stop=(k == K - 1), skip_group_check=True)
                last.then_inc(win_mm, 1)

            def win_chan(b):
                for c in range(2):
                    for k in range(K):
                        last = mm(bank[b][:, c * T:(c + 1) * T], RING[b][:, k, c * P:(c + 1) * P], HT[:, k, :],
                                  start=(k == 0), stop=(k == K - 1), skip_group_check=True)
                last.then_inc(win_mm, 1)

            def channel_sums(weights, src, banks):
                flat = src.rearrange("p a b -> p (a b)")
                for i, bk in enumerate(banks):
                    last = mm(bank[bk][:], weights, flat[:, i * 512:(i + 1) * 512], start=True, stop=True)
                return last

            def product(p, bk, f):
                for q in range(4):
                    lhs, rhs = f(q)
                    last = mm(bank[bk][:, q * P:(q + 1) * P], lhs, rhs, start=True, stop=True, skip_group_check=True)
                last.then_inc(prod_mm, 1)

            def low_rank_and_ab():
                pe.wait_ge(ab_in, 16)
                for a in range(TT):
                    for k in range(K):
                        last = mm(bank[3][:, a * 12:(a + 1) * 12], HT[:, k, a * P:(a + 1) * P], WAB[:, k, :],
                                  start=(k == 0), stop=(k == K - 1), skip_group_check=True)
                last.then_inc(ab_mm, 1)
                pe.wait_ge(lora_in, 32)
                pe.wait_ge(xwa_ok, 1)
                for f, src in enumerate((XW, XA)):
                    for k in range(K):
                        last = mm(bank[4][0:96, f * T:(f + 1) * T], L1[:, f, k, :], src[:, k, :],
                                  start=(k == 0), stop=(k == K - 1), skip_group_check=True)
                last.then_inc(lo_mm, 1)

            def low_rank_out():
                for f in range(2):
                    for half in range(3):
                        u = f * 3 + half
                        if u == 3:
                            pe.wait_ge(sig_ok, 1)
                        for jj in range(2):
                            j = half * 2 + jj
                            last = mm(bank[5 + half][:, jj * T:(jj + 1) * T], L2[0:96, f, j * P:(j + 1) * P], LH[0:96, f, :],
                                      start=True, stop=True, skip_group_check=True)
                        last.then_inc(lo2_mm, 1)

            def retention_turn():
                pe.wait_ge(rot_ok, 1)
                pe.wait_ge(ab_ok, 1)
                pe.wait_ge(lo_ok, 1)
                for u, src in enumerate((QR, KR)):
                    for a in range(TT):
                        for h in range(RH):
                            last = nc.tensor.transpose(bank[3 + 2 * u + a][:, h * P:(h + 1) * P], src[:, a, h * P:(h + 1) * P], ident)
                last.then_inc(rt_mm, 1)
                pe.wait_ge(rt_ok, 1)

            def retention_scores():
                pe.wait_ge(sig_ok, 2)
                for a, bk in ((0, 7), (1, 3)):
                    for h in range(RH):
                        mm(bank[bk][:, h * P:(h + 1) * P], KT[:, a, h, :], QT[:, a, h, :], start=True, stop=True, skip_group_check=True)
                for h in range(RH):
                    last = mm(bank[4][:, h * P:(h + 1) * P], KD0[:, h * P:(h + 1) * P], TM[:, 0, 2 * RT + h * P:2 * RT + (h + 1) * P],
                              start=True, stop=True, skip_group_check=True)
                last.then_inc(rt_mm, 1)

            def retention_values():
                pe.wait_ge(rt_dve, 1)
                for a in range(TT):
                    for h in range(RH):
                        mm(bank[5 + a][:, h * P:(h + 1) * P], ST[:, a, h, :], TM[:, a, 2 * RT + h * P:2 * RT + (h + 1) * P],
                           start=True, stop=True, skip_group_check=True)
                for h in range(RH):
                    last = mm(bank[7][:, h * P:(h + 1) * P], QT[:, 1, h, :], KV0[:, h * P:(h + 1) * P],
                              start=True, stop=True, skip_group_check=True)
                last.then_inc(rt_mm, 1)

            def gate_sums():
                pe.wait_ge(gate_ok, 1)
                for a in range(TT):
                    mm(bank[6][:, a * 6:a * 6 + 6], con("incl"), gate[:, a * 6:a * 6 + 6], start=True, stop=True, skip_group_check=True)
                    mm(bank[6][:, 12 + a * 6:12 + a * 6 + 6], con("after"), gate[:, a * 6:a * 6 + 6], start=True, stop=True, skip_group_check=True)
                for m in range(12):
                    last = mm(bank[3 + m // 4][:, (m % 4) * P:(m % 4 + 1) * P], GTMP1[:, m, :], con("incl"), start=True, stop=True, skip_group_check=True)
                last.then_inc(gate_mm, 1)

            def beta_rows():
                pe.wait_ge(gexp_ok, 1)
                for m in range(12):
                    last = mm(bank[3 + m // 4][:, (m % 4) * P:(m % 4 + 1) * P], GTMP2[:, m, :], ident, start=True, stop=True, skip_group_check=True)
                last.then_inc(gate_mm, 1)

            def gdn_lengths(i):
                pe.wait_ge(conv_ok, i + 1)
                if i:
                    pe.wait_ge(gn_ok, i)
                else:
                    pe.wait_ge(gexp_ok, 2)
                channel_sums(con("ones"), CSQ, (3, 4, 5)).then_inc(sq_mm, 1)

            def kk_lengths():
                pe.wait_ge(sq_ok, 1)
                pe.wait_ge(gn_ok, 2)
                channel_sums(con("bd"), T2, (3, 4, 5)).then_inc(sq_mm, 1)

            def gdn_products():
                pe.wait_ge(gn_ok, 2)
                pe.wait_ge(exp_ok, 2)
                p = 0
                for g in range(3):
                    for rhs in (gq, gk):
                        if p >= 5:
                            pe.wait_ge(prod_ok, p - 4)

                        def pair(q, g=g, rhs=rhs):
                            h, a = 2 * g + q // 2, q % 2
                            return gk[:, h, a * P:(a + 1) * P], rhs[:, h, a * P:(a + 1) * P]
                        product(p, 3 + p % 5, pair)
                        p += 1

            after = {NTOK - 1: (low_rank_and_ab, retention_turn, low_rank_out, retention_scores),
                     NTOK + 2: (retention_values,), NTOK + 5: (gate_sums,), NTOK + 8: (beta_rows,),
                     NTOK + 10: (lambda: gdn_lengths(0),), NTOK + 13: (lambda: gdn_lengths(1),),
                     NTOK + 20: (kk_lengths,), NTOK + 23: (gdn_products,)}
            for n in range(NCHUNK):
                if n >= 3:
                    pe.wait_ge(win_out, n - 2)
                pe.wait_ge(win_in[n % 3], 16 * (n // 3 + 1))
                (win_token if n < NTOK else win_chan)(n % 3)
                for step in after.get(n, ()):
                    step()
            pe.wait_ge(bon_ok, 1)
            pe.wait_ge(prod_ok, 6)
            channel_sums(con("bd"), T4, (3, 4, 5)).then_inc(bon_mm, 1)

            def to_tokens(u, src):
                for a in range(TT):
                    if u + a >= 4:
                        pe.wait_ge(tok_a, min(u + a - 3, 8))
                    for j in range(6):
                        bk = bank[2 * ((u + a) % 4) + j // 4]
                        last = nc.tensor.transpose(bk[:, (j % 4) * P:(j % 4 + 1) * P], src[:, j, a * P:(a + 1) * P], ident)
                    last.then_inc(tok_mm, 1)

            pe.wait_ge(chan_ok, 1)
            pe.wait_ge(win_out, 32)
            for u, src in ((0, T3), (2, T5), (4, pv), (6, T1)):
                to_tokens(u, src)

            pe.wait_ge(tok_a, 8)
            p = 6
            for u, src in ((8, gk), (10, gv)):
                to_tokens(u, src)
            pe.wait_ge(tok_d, 4)

            for bt in range(3):
                if bt:
                    pe.wait_ge(u2_ok, bt)
                if bt < 2:
                    hh = bt
                    rows = slice(hh * CH, (hh + 1) * CH)
                    for g in range(3):
                        for lhs, rhs in ((T2, T1), (pk, T1), (T2, pr), (pk, pr)):
                            def pair(q, g=g, lhs=lhs, rhs=rhs):
                                j, a = 2 * g + q // 2, q % 2
                                return lhs[rows, j, a * P:(a + 1) * P], rhs[rows, j, a * P:(a + 1) * P]
                            if p >= 14:
                                pe.wait_ge(prod_ok, p - 7)
                            product(p, p % 8, pair)
                            p += 1
                    pe.wait_ge(prod_ok, p)
                pe.wait_ge(t0_ok, bt + 1)
                for g in range(3):
                    for q in range(4):
                        last = nc.tensor.transpose(bank[2 * g + 1][:, q * P:(q + 1) * P], TI3[:, g, q * P:(q + 1) * P], ident)
                    last.then_inc(t0_mm, 1)
                for lv in range(1, LEVELS):
                    n = (bt * (LEVELS - 1) + lv - 1) * 3
                    for g in range(3):
                        pe.wait_ge(lm_ok, n + g + 1)
                        if lv == 1:
                            pe.wait_ge(t0_sb, 3 * bt + g + 1)
                        elif lv > 1:
                            pe.wait_ge(t_ok, n - 3 + g + 1)
                        for q in range(4):
                            c = slice(q * P, (q + 1) * P)
                            last = mm(bank[2 * g][:, c], LM3[:, g, c], TM3[:, g, c], start=True, stop=True, skip_group_check=True)
                        last.then_inc(a_mm, 1)
                    for g in range(3):
                        pe.wait_ge(a_sb, n + g + 1)
                        for q in range(4):
                            c = slice(q * P, (q + 1) * P)
                            if lv < LEVELS - 1:
                                mm(bank[2 * g + 1][:, c], TI3[:, g, c], AS3[:, g, c], start=True, stop=True, skip_group_check=True)
                            last = mm(bank[2 * g][:, c], AS3[:, g, c], TI3[:, g, c], start=True, stop=True, skip_group_check=True)
                        last.then_inc(t_mm, 1)
                pe.wait_ge(t_ok, 3 * (LEVELS - 1) * (bt + 1))
                if bt < 2:
                    for g in range(3):
                        for q in range(4):
                            j, a = 2 * g + q // 2, q % 2
                            c0 = (g % 2) * 256 + q * CH
                            last = mm(bank[g // 2][:, c0:c0 + CH], LK3[:, g, q * P:(q + 1) * P],
                                      tok(T3)[:, a, j * P + hh * CH:j * P + (hh + 1) * CH],
                                      start=True, stop=True, skip_group_check=True)
                    last.then_inc(u1_mm, 1)
                    pe.wait_ge(u1_ok, bt + 1)
                    for g in range(3):
                        for q in range(4):
                            j, a = 2 * g + q // 2, q % 2
                            c0 = (g % 2) * 256 + q * CH
                            mm(bank[2 + g // 2][:, c0:c0 + CH], TI3[:, g, q * P:(q + 1) * P], X1[:, g, q * CH:(q + 1) * CH],
                               start=True, stop=True, skip_group_check=True)
                            last = mm(bank[4 + g][rows, q * P:(q + 1) * P],
                                      tok(T5)[:, a, j * P + hh * CH:j * P + (hh + 1) * CH], TI3[:, g, q * P:(q + 1) * P],
                                      start=True, stop=True, skip_group_check=True)
                    last.then_inc(u2_mm, 1)
                else:
                    for g in range(3):
                        for q in range(4):
                            h, a = 2 * g + q // 2, q % 2
                            m = h * 2 + a
                            mm(bank[2 * a + h // 4][:, (h % 4) * P:(h % 4 + 1) * P], TI3[:, g, q * P:(q + 1) * P],
                               VBG[:, a, h * P:(h + 1) * P], start=True, stop=True, skip_group_check=True)
                            last = mm(bank[4 + m // 4][:, (m % 4) * P:(m % 4 + 1) * P], tok(gk)[:, a, h * P:(h + 1) * P],
                                      TI3[:, g, q * P:(q + 1) * P], start=True, stop=True, skip_group_check=True)
                    last.then_inc(u2_mm, 1)
            pe.wait_ge(u2_ok, 3)

            kinds = ((0, T1, M1, pr), (2, WTG, S1, gq))
            for c in range(NC):
                a, base = c // 2, CH * (c % 2)
                rows, cols_ = slice(base, base + CH), slice(a * P + base, a * P + base + CH)
                pe.wait_ge(m_ok, c + 1)
                for b0, wt, st, _ in kinds:
                    for j in range(6):
                        last = mm(bank[b0 + j // 4][rows, (j % 4) * P:(j % 4 + 1) * P], wt[:, j, cols_], st[:, j, :],
                                  start=True, stop=True, skip_group_check=True)
                last.then_inc(su_mm, 1)
                if c == 2:
                    pe.wait_ge(so_ok, 1)
                for b0, _, st, rd in kinds:
                    for j in range(6):
                        last = mm(bank[4 + b0 + j // 4][rows, (j % 4) * P:(j % 4 + 1) * P], rd[:, j, cols_], st[:, j, :],
                                  start=(j % 4 == 0), stop=False, skip_group_check=True)
                last.then_inc(sx_mm, 1)
                pe.wait_ge(su_ok, c + 1)
                if c < NC - 1:
                    for j in range(6):
                        o = bank[j // 4][:, (j % 4) * P:(j % 4 + 1) * P]
                        cj = slice(j * P, (j + 1) * P)
                        mm(o, tok(T6)[rows, a, cj], tok(T2)[rows, a, cj], start=(j % 4 == 0), stop=False, skip_group_check=True)
                        mm(o, tok(T7)[rows, a, cj], tok(T3)[rows, a, cj], start=False, stop=True, skip_group_check=True)
                    for j in range(6):
                        cj = slice(j * P, (j + 1) * P)
                        last = mm(bank[2 + j // 4][:, (j % 4) * P:(j % 4 + 1) * P], KDG[rows, a, cj], VBG[rows, a, cj],
                                  start=True, stop=True, skip_group_check=True)
                    last.then_inc(sm_mm, 1)
                if c % 2:
                    for j in range(6):
                        for hh in range(2):
                            g, q = hh * 3 + j // 2, (j % 2) * 2 + a
                            cj = slice(j * P + hh * CH, j * P + (hh + 1) * CH)
                            o = bank[4 + j // 4][:, (j % 4) * P + hh * CH:(j % 4) * P + (hh + 1) * CH]
                            mm(o, RB[:, g, q * P:(q + 1) * P], tok(T2)[:, a, cj], start=False, stop=False, skip_group_check=True)
                            mm(o, RK[:, g, q * P:(q + 1) * P], tok(T3)[:, a, cj], start=False, stop=True, skip_group_check=True)
                    for h in range(6):
                        last = mm(bank[6 + h // 4][:, (h % 4) * P:(h % 4 + 1) * P], DT[:, h * 2 + a, :],
                                  VBG[:, a, h * P:(h + 1) * P], start=False, stop=True, skip_group_check=True)
                    last.then_inc(so_mm, 1)

            def head_transposes(b0, n, src):
                for j in range(n):
                    for a in range(TT):
                        o = (j % 2) * T + a * P
                        last = nc.tensor.transpose(bank[b0 + j // 2][:, o:o + P], src(a, j), ident)
                last.then_inc(mt_mm, 1)

            pe.wait_ge(o_ok, 1)
            pe.wait_ge(so_ok, 2)
            head_transposes(0, 6, lambda a, j: tok(pk)[:, a, j * P:(j + 1) * P])
            pe.wait_ge(o_ok, 2)
            head_transposes(3, 6, lambda a, j: OG[:, a, j * P:(j + 1) * P])
            head_transposes(6, 4, lambda a, j: YR[:, a * RH + j, :])

            pe.wait_ge(mt_ok, 3)
            for k in range(K):
                pe.wait_ge(wo_in[k % 6], 16 * (k // 6 + 1))
                for a in range(TT):
                    for n in range(4):
                        last = mm(bank[a * 4 + n][:], MIX[:, k, a * P:(a + 1) * P], WO[k % 6][:, n * 512:(n + 1) * 512],
                                  start=(k == 0), stop=(k == K - 1))
                last.then_inc(wo_mm, 1)

            pe.wait_ge(xs_ok, 1)
            xs = XS.rearrange("p a (d k) -> p a k d", k=K)
            for r in range(8):
                if r >= 4:
                    pe.wait_ge(xs_t, r - 3)
                for kk in range(2):
                    for a in range(TT):
                        o = kk * T + a * P
                        last = nc.tensor.transpose(bank[r % 4][:, o:o + P], xs[:, a, 2 * r + kk, :], ident)
                last.then_inc(xs_mm, 1)
            pe.wait_ge(xs_t, 8)
            pe.wait_ge(rw_in, 16)
            for a in range(TT):
                for k in range(K):
                    last = mm(bank[4 + a][:, 0:36], XTT[:, k, a * P:(a + 1) * P], RWT[:, k, :], start=(k == 0), stop=(k == K - 1))
            last.then_inc(lg_mm, 1)
            pe.wait_ge(e_ok, 1)
            mm(bank[6][:, 0:32], con("before"), R1[:, 0, :], start=True, stop=True, skip_group_check=True)
            mm(bank[6][:, 32:64], con("ones"), R1[:, 0, :], start=True, stop=False, skip_group_check=True)
            mm(bank[6][:, 32:64], con("before"), R1[:, 1, :], start=False, stop=True, skip_group_check=True)
            mm(bank[6][:, 64:96], con("ones"), R1[:, 0, :], start=True, stop=False, skip_group_check=True)
            mm(bank[6][:, 64:96], con("ones"), R1[:, 1, :], start=False, stop=True, skip_group_check=True).then_inc(pos_mm, 1)

            def experts(r):
                pe.wait_ge(p_ok, r + 1)
                pe.sem_inc(wu_free[0], 1)
                pe.sem_inc(wd_free[0], 1)
                for i in range(4):
                    for qd in range(2):
                        for a in range(TT):
                            o = qd * T + a * P
                            last = nc.tensor.transpose(bank[i][:, o:o + P], PG[:, a, (2 * i + qd) * P:(2 * i + qd + 1) * P], ident)
                    last.then_inc(sg_mm, 1)
                for n in range(2 * K):
                    k, half = n // 2, n % 2
                    if n >= 4:
                        pe.wait_ge(g_act if n % 2 == 0 else g_dve, r * K + ((n - 4) // 2 + 1))
                    for a in range(TT):
                        last = mm(bank[4 + n % 4][:], xs[:, a, k, :], PS[:, a, half * 512:(half + 1) * 512],
                                  start=(a == 0), stop=(a == TT - 1))
                    last.then_inc(g_mm, 1)
                pe.wait_ge(g_act, r * K + K)
                pe.wait_ge(g_dve, r * K + K)
                pe.wait_ge(sg_ok, r * 4 + 4)
                pe.wait_ge(xs_out, 16)
                pe.sem_inc(wu_free[1], 1)
                pe.sem_inc(wd_free[1], 1)
                with pe.Fori(0, 8) as i:
                    def up(b):
                        s = b % 2
                        pe.wait_ge(wu_in[s], (r * 16 + i * 2) * 32 + 32 * (b // 2 + 1))
                        pe.wait_ge(xe_ok, r * NE + i * 4 + (b + 1))
                        if b >= 2:
                            pe.wait_ge(up_sb, r * NE + i * 4 + (b - 1))
                        for k in range(K):
                            j = k % 4
                            for w in range(2):
                                last = mm(bank[s][32 * j:32 * j + 32, w * HID:(w + 1) * HID], XE[s][:, k, :], WU[s][:, w, k, :],
                                          start=(k < 4 and w == 0), stop=(k >= 12), skip_group_check=True)
                        last.then_inc(up_mm, 1)
                        pe.wait_ge(up_mm, r * NE + i * 4 + (b + 1))
                        pe.sem_inc(wu_free[s], 1)

                    def hidden(b):
                        pe.wait_ge(up_sb, r * NE + i * 4 + (b + 1))
                        if b >= 1:
                            pe.wait_ge(hd_ok, r * NE + i * 4 + b)
                        for c in range(4):
                            last = mm(bank[2][:, c * TOPC:(c + 1) * TOPC], UP[b % 2][:, c * P:(c + 1) * P], stack,
                                      start=True, stop=True, skip_group_check=True)
                        last.then_inc(h_mm, 1)

                    def down(b):
                        s = b % 2
                        pe.wait_ge(hd_ok, r * NE + i * 4 + (b + 1))
                        pe.wait_ge(wd_in[s], (r * 16 + i * 2) * 16 + 16 * (b // 2 + 1))
                        for n in range(4):
                            for f in range(2):
                                last = mm(bank[3 + n][32 * b:32 * b + 32, :], HD[s][:, f, :], WD[s][:, f, n * 512:(n + 1) * 512],
                                          start=(f == 0), stop=(f == 1), skip_group_check=True)
                        last.then_inc(dn_mm, 1)
                        pe.wait_ge(dn_mm, r * NE + i * 4 + (b + 1))
                        pe.sem_inc(wd_free[s], 1)

                    up(0)
                    up(1)
                    hidden(0)
                    down(0)
                    up(2)
                    hidden(1)
                    down(1)
                    up(3)
                    hidden(2)
                    down(2)
                    hidden(3)
                    down(3)
                    pe.wait_ge(sgq_ok, r * 8 + i + 1)
                    pe.wait_ge(ya_ok, r * 8 + i + 1)
                    pe.wait_ge(yd_ok, r * 8 + i + 1)
                    for q in range(8):
                        a, n = q // 4, q % 4
                        if q >= 2:
                            pe.wait_ge(sc_ok, (r * 8 + i) * 8 + (q - 1))
                        mm(bank[7 if q % 2 else 2][:], SGQ[:, a * P:(a + 1) * P], YS[:, n * 512:(n + 1) * 512],
                           start=True, stop=True).then_inc(sc_mm, 1)
                    pe.wait_ge(sc_ok, (r * 8 + i) * 8 + 8)

            experts(0)
            pe.wait_ge(flag_ok, 1)
            with pe.If(pe.value_load(flag[0:1, 0:1]) == 1):
                with pe.Fori(1, PASSES) as r:
                    experts(r)

        @block.scalar
        def _(eng):
            f = nc.scalar.activation
            done = Steps(eng, act)
            cp = ACT.Copy

            def root(n, ap):
                eng.wait_ge(ss_ok, n)
                f(ap, ap, ACT.Sqrt).then_inc(std_ok, 1)

            root(1, rstd)
            eng.wait_ge(ang_ok, 1)
            done(f(SIN, ANG, ACT.Sin))
            f(COS, ANR, ACT.Sin).then_inc(sin_ok, 1)

            eng.wait_ge(xt_mm, 8)

            def evac(n):
                eng.wait_ge(win_mm, n + 1)
                if n < NTOK:
                    f(TM[:, :, n * CW:(n + 1) * CW], bank[n % 3][:].rearrange("p (a c) -> p a c", a=TT), cp).then_inc(win_out, 1)
                else:
                    t = SEGMENTS[(n - NTOK) // 3][0] + 2 * ((n - NTOK) % 3)
                    f(PJ[:, t:t + 2, :].rearrange("p a b -> p (a b)"), bank[n % 3][:], cp).then_inc(win_out, 1)

            def low_rank():
                eng.wait_ge(ab_mm, 1)
                f(AB, bank[3][:, 0:24].rearrange("p (a c) -> p a c", a=TT), cp).then_inc(ab_ok, 1)
                eng.wait_ge(lo_mm, 1)
                done(f(LH[0:96, 0, :], bank[4][0:96, 0:T], ACT.Tanh))
                f(LH[0:96, 1, :], bank[4][0:96, T:2 * T], cp).then_inc(lo_ok, 1)

            def retention_turned():
                eng.wait_ge(rt_mm, 1)
                for u, dst in enumerate((QT, KT)):
                    for a in range(TT):
                        done(f(dst[:, a].rearrange("p h c -> p (h c)"), bank[3 + 2 * u + a][:], cp))
                eng.sem_inc(rt_ok, 1)

            def low_rank_gates():
                for u in range(6):
                    fct, half = u // 3, u % 3
                    eng.wait_ge(lo2_mm, u + 1)
                    for jj in range(2):
                        j = half * 2 + jj
                        done(f((T3, T4)[fct][:, j, :], bank[5 + half][:, jj * T:(jj + 1) * T], ACT.Sigmoid,
                               bias=pcol(("w0", "a0")[fct], j)))
                    if half == 2:
                        eng.sem_inc(sig_ok, 1)

            def retention_inner():
                eng.wait_ge(rt_mm, 3)
                for a in range(TT):
                    done(f(YR[:, a * RH:(a + 1) * RH, :].rearrange("p h c -> p (h c)"), bank[5 + a][:], cp))
                eng.sem_inc(rt_ok, 1)

            def gate_functions():
                eng.wait_ge(ga_ok, 1)
                done(f(stat[:, 0:12], stat[:, 0:12], ACT.Exp, scale=-1.0))
                done(f(ea, pcol("alog", 0, 6), ACT.Exp))
                done(f(stat[:, 0:12], stat[:, 0:12], ACT.Ln, bias=1.0))
                done(f(beta.rearrange("p (a b) -> p a b", a=TT), AB[:, :, 6:12], ACT.Sigmoid))
                eng.sem_inc(gb_ok, 1)

            def gate_exps():
                eng.wait_ge(gexp_in, 1)
                done(f(DT, DT, ACT.Exp))
                done(f(egc, gcum, ACT.Exp))
                done(f(ekd, bank[6][:, 12:24], ACT.Exp))
                eg = EG.rearrange("p a b -> p (a b)")
                for i in range(3):
                    done(f(eg[:, i * 512:(i + 1) * 512], bank[3 + i][:], ACT.Exp))
                eng.sem_inc(gexp_ok, 1)

            def conv_silu(s):
                eng.wait_ge(conv_in, s + 1)
                f((gq, gk, gv)[s], CACC, ACT.Silu).then_inc(silu_ok, 1)

            def lengths(n, dst, ok):
                eng.wait_ge(sq_mm, n)
                flat = dst.rearrange("p a b -> p (a b)")
                for i in range(3):
                    done(f(flat[:, i * 512:(i + 1) * 512], bank[3 + i][:], ACT.Sqrt, bias=eps6))
                eng.sem_inc(ok, 1)

            def rwkv_decays():
                eng.wait_ge(cum_ok, 1)
                done(f(T6, T6, ACT.Exp, scale=-DECAY))
                done(f(T7, T5, ACT.Exp, scale=-DECAY))
                done(f(T3, T5, ACT.Exp, scale=DECAY))
                eng.sem_inc(exp_ok, 1)

            after = {NTOK - 1: (low_rank, retention_turned, low_rank_gates), NTOK + 2: (retention_inner,),
                     NTOK + 3: (lambda: root(2, stat2[:, 0:8]),), NTOK + 4: (gate_functions,),
                     NTOK + 5: (lambda: conv_silu(0), ), NTOK + 7: (gate_exps,),
                     NTOK + 11: (lambda: lengths(1, CSQ, gs_root), lambda: conv_silu(1)),
                     NTOK + 14: (lambda: lengths(2, CSQ, gs_root), lambda: conv_silu(2)),
                     NTOK + 16: (rwkv_decays,), NTOK + 21: (lambda: lengths(3, T2, exp_ok),)}
            for n in range(NCHUNK):
                evac(n)
                for step in after.get(n, ()):
                    step()
            eng.wait_ge(win_out, NCHUNK)
            for u, dst in enumerate((T6, T6, T7, T7, T3, T3, T5, T5)):
                eng.wait_ge(tok_mm, u + 1)
                b0 = 2 * (u % 4)
                if u == 6:
                    eng.wait_ge(bon_done, 1)
                done(f(tok(dst)[:, u % 2, 0:512], bank[b0][:], cp))
                done(f(tok(dst)[:, u % 2, 512:768], bank[b0 + 1][:, 0:256], cp))
                eng.sem_inc(tok_a, 1)
            eng.wait_ge(chan_ok, 1)
            done(f(pg, pg, ACT.Sigmoid))
            done(f(gz, gz, ACT.Silu))
            done(f(rg, rg, ACT.Silu))
            eng.sem_inc(gates_ok, 1)
            for bt in range(3):
                for g in range(3):
                    eng.wait_ge(t0_mm, bt * 3 + g + 1)
                    f(TM3[:, g, :], bank[2 * g + 1][:], cp).then_inc(t0_sb, 1)
                for lv in range(1, LEVELS):
                    n = (bt * (LEVELS - 1) + lv - 1) * 3
                    for g in range(3):
                        eng.wait_ge(a_mm, n + g + 1)
                        f(AS3[:, g, :], bank[2 * g][:], cp).then_inc(a_sb, 1)
                if bt < 2:
                    rows = slice(bt * CH, (bt + 1) * CH)
                    eng.wait_ge(u1_mm, bt + 1)
                    x1 = X1.rearrange("p a b -> p (a b)")
                    done(f(x1[:, 0:512], bank[0][:], cp, scale=-1.0))
                    done(f(x1[:, 512:768], bank[1][:, 0:256], cp, scale=-1.0))
                    eng.sem_inc(u1_ok, 1)
                    eng.wait_ge(u2_mm, bt + 1)
                    u0 = tok(pv).rearrange("p a (j h c) -> p a j h c", j=NJ, h=2)
                    for g in range(3):
                        ps = bank[2 + g // 2][:, (g % 2) * 256:(g % 2) * 256 + 256].rearrange("p (j a c) -> p j a c", j=2, a=TT)
                        for a in range(TT):
                            done(f(u0[:, a, 2 * g:2 * g + 2, bt, :], ps[:, :, a, :], cp))
                        done(f(T1[rows, 2 * g:2 * g + 2, :].rearrange("p a b -> p (a b)"), bank[4 + g][rows, :], cp))
                    eng.sem_inc(u2_ok, 1)
                else:
                    eng.wait_ge(u2_mm, 3)
                    for a in range(TT):
                        done(f(tok(gv)[:, a, 0:512], bank[2 * a][:], cp))
                        done(f(tok(gv)[:, a, 512:768], bank[2 * a + 1][:, 0:256], cp))
                    wt = WTG.rearrange("p a b -> p (a b)")
                    for i in range(3):
                        done(f(wt[:, i * 512:(i + 1) * 512], bank[4 + i][:], cp))
                    eng.sem_inc(u2_ok, 1)
            for a in range(TT):
                eng.wait_ge(so_mm, a + 1)
                for b0, dst in ((4, tok(pk)), (6, OG)):
                    done(f(dst[:, a, 0:512], bank[b0][:], cp))
                    done(f(dst[:, a, 512:768], bank[b0 + 1][:, 0:256], cp))
                eng.sem_inc(so_ok, 1)
            root(3, stat2)
            root(4, stat[:, 0:12])
            root(5, rstd)
            eng.wait_ge(rex_in, 1)
            f(R2[:, :, 0:4], R1[:, :, 0:4], ACT.Exp).then_inc(rex_ok, 1)
            eng.wait_ge(rex_in, 2)
            f(stat2[:, 0:2], stat2[:, 0:2], ACT.Exp).then_inc(rex_ok, 1)

            def experts(r):
                for i in range(4):
                    eng.wait_ge(sg_mm, r * 4 + (i + 1))
                    f(SG[:, 2 * i:2 * i + 2, :].rearrange("p a b -> p (a b)"), bank[i][:], cp).then_inc(sg_ok, 1)
                for k in range(K):
                    eng.wait_ge(g_mm, r * 32 + (2 * k + 1))
                    f(XT[:, k, 0:512], bank[4 + (2 * k) % 4][:], cp, scale=pcol("norm2", k)).then_inc(g_act, 1)
                with eng.Fori(0, 8) as i:
                    def up_copy(b):
                        eng.wait_ge(up_mm, r * NE + i * 4 + (b + 1))
                        if b >= 2:
                            eng.wait_ge(h_mm, r * NE + i * 4 + (b - 1))
                        f(UP[b % 2], bank[b % 2][:], cp).then_inc(up_sb, 1)

                    def silu(b):
                        eng.wait_ge(h_mm, r * NE + i * 4 + (b + 1))
                        if b >= 1:
                            eng.wait_ge(hd_ok, r * NE + i * 4 + b)
                        f(GS, bank[2][:, 0:64], ACT.Silu).then_inc(gs_ok, 1)

                    up_copy(0)
                    up_copy(1)
                    silu(0)
                    up_copy(2)
                    silu(1)
                    up_copy(3)
                    silu(2)
                    silu(3)
                    eng.wait_ge(dn_mm, r * NE + i * 4 + 4)
                    f(YS[:, 0:512], bank[3][:], cp).then_inc(ya_half, 1)
                    eng.wait_ge(ya_half, r * 8 + i + 1)
                    f(YS[:, 512:1024], bank[4][:], cp).then_inc(ya_ok, 1)

            experts(0)
            eng.wait_ge(flag_ok, 1)
            with eng.If(eng.value_load(flag[0:1, 0:1]) == 1):
                with eng.Fori(1, PASSES) as r:
                    experts(r)
            root(6, rstd)

        @block.vector
        def _(eng):
            v = nc.vector
            done = Steps(eng, dve)
            tt, ts, stt = v.tensor_tensor, v.tensor_scalar, v.scalar_tensor_tensor
            MUL, ADD, SUB, MAX, MIN, EQ = ALU.mult, ALU.add, ALU.subtract, ALU.max, ALU.min, ALU.is_equal

            def rms(n, src, junk):
                for a in range(TT):
                    done(v.tensor_tensor_reduce(junk(a), src[:, a], src[:, a], 1.0, 0.0, MUL, ADD, ssq[:, a:a + 1]))
                done(ts(rstd, ssq, 1.0 / D, 1e-6, MUL, ADD))
                eng.sem_inc(ss_ok, 1)
                eng.wait_ge(std_ok, n)
                done(v.reciprocal(rstd, rstd))

            done(v.memset(eps6, 1e-6))
            eng.wait_ge(x_in, 16)
            rms(1, X, lambda a: XN[:, a])
            for a in range(TT):
                done(ts(XN[:, a], X[:, a], rstd[:, a:a + 1], None, MUL))
            eng.sem_inc(xn_ok, 1)
            eng.wait_ge(c_in, 48)
            for r in range(8):
                eng.wait_ge(xt_mm, r + 1)
                for kk in range(2):
                    k = 2 * r + kk
                    done(ts(HT[:, k, :], bank[3 + r % 4][:, kk * T:(kk + 1) * T], pcol("norm1", k), None, MUL))
                eng.sem_inc(ht_ok, 1)

            done(v.tensor_copy(posf, posi[:]))
            c1 = 6.28125
            c2 = round((2 * np.pi - c1) * 2 ** 19) / 2 ** 19
            c3 = 2 * np.pi - c1 - c2
            magic = 1.5 * 2 ** 23
            turns = RTMP[:, 0:P].rearrange("p (a b) -> p a b", a=TT)
            for a in range(TT):
                done(ts(ANG[:, a], con("freq"), posf[:, a:a + 1], None, MUL))
            done(v.tensor_copy(ANR, ANG))
            for dst, quarter in ((ANR, 0.25), (ANG, 0.0)):
                done(ts(turns, dst, 1.0 / (2 * np.pi), quarter, MUL, ADD))
                done(ts(turns, turns, magic, None, ADD))
                done(ts(turns, turns, magic, None, SUB))
                for c in (c1, c2, c3):
                    done(stt(dst, turns, -c, dst, MUL, ADD))
                done(ts(dst, dst, quarter * 2 * np.pi, None, ADD))
                done(ts(dst, dst, PI_LO, -PI_LO, MIN, MAX))
            eng.sem_inc(ang_ok, 1)

            done(tt(DH[:, :, 1:T], HT[:, :, 0:T - 1], HT[:, :, 1:T], SUB))
            done(ts(DH[:, :, 0:1], HT[:, :, 0:1], -1.0, None, MUL))
            for name, dst in (("mu_w", XW), ("mu_a", XA)):
                for k in range(K):
                    done(stt(dst[:, k, :], DH[:, k, :], pcol(name, k), HT[:, k, :], MUL, ADD))
            eng.sem_inc(xwa_ok, 1)

            eng.wait_ge(win_out, NTOK)
            eng.wait_ge(sin_ok, 1)
            tmp = RTMP[:, 0:256].rearrange("p (h c) -> p h c", h=RH)
            for src, dst in ((0, QR), (RT, KR)):
                for a in range(TT):
                    s = TM[:, a, src:src + RT].rearrange("p (h e c) -> p h e c", h=RH, e=2)
                    o = dst[:, a].rearrange("p (h e c) -> p h e c", h=RH, e=2)
                    cos, sin = over(COS[:, a], RH), over(SIN[:, a], RH)
                    for e, op in ((0, SUB), (1, ADD)):
                        done(tt(o[:, :, e, :], s[:, :, e, :], cos, MUL))
                        done(tt(tmp, s[:, :, 1 - e, :], sin, MUL))
                        done(tt(o[:, :, e, :], o[:, :, e, :], tmp, op))
            for h in range(RH):
                done(ts(KD0[:, h * P:(h + 1) * P], KR[:, 0, h * P:(h + 1) * P], con("kdec")[:, h:h + 1], None, MUL))
            eng.sem_inc(rot_ok, 1)
            eng.wait_ge(rt_mm, 2)
            for a, bk in ((0, 7), (1, 3)):
                done(tt(ST[:, a].rearrange("p h c -> p (h c)"), bank[bk][:], con("dmask"), MUL))
            done(v.tensor_copy(KV0, bank[4][:]))
            eng.sem_inc(rt_dve, 1)
            eng.wait_ge(rt_ok, 2)
            for h in range(RH):
                done(stt(YR[:, RH + h, :], bank[7][:, h * P:(h + 1) * P], con("qdec")[:, h:h + 1], YR[:, RH + h, :], MUL, ADD))

            def head_norm(n, y, sq, g, w, st, mean, eps):
                if mean:
                    done(v.tensor_reduce(st, y, AX, ADD))
                    done(ts(st, st, 1.0 / w, None, MUL))
                    done(tt(y, y, wide(st, w), SUB))
                done(tt(sq, y, y, MUL))
                done(v.tensor_reduce(st, sq, AX, ADD))
                done(ts(st, st, 1.0 / w, eps, MUL, ADD))
                eng.sem_inc(ss_ok, 1)
                eng.wait_ge(std_ok, n)
                done(v.reciprocal(st, st))
                done(tt(y, y, wide(st, w), MUL))

            head_norm(2, YR, view(198, 8, P), 8, P, stat2[:, 0:8], True, 1e-5)

            g3 = gate.rearrange("p (a b) -> p a b", a=TT)
            eng.wait_ge(ab_ok, 1)
            done(tt(g3, AB[:, :, 0:6], over(pcol("dt", 0, 6), TT), ADD))
            done(ts(stat[:, 0:12], gate, -1.0, None, MUL))
            done(tt(stat[:, 0:12], stat[:, 0:12], gate, MAX))
            eng.sem_inc(ga_ok, 1)
            eng.wait_ge(gb_ok, 1)
            done(stt(gate, gate, 0.0, stat[:, 0:12], MAX, ADD))
            done(stt(g3, g3, -1.0, over(ea, TT), MUL, MUL))
            g1v = GTMP1.rearrange("p (h a) c -> p h a c", a=TT)
            g2v = GTMP2.rearrange("p (h a) c -> p h a c", a=TT)
            for a in range(TT):
                done(v.tensor_copy(g1v[:, :, a, :], wide(gate[:, a * 6:a * 6 + 6], P)))
                done(v.tensor_copy(g2v[:, :, a, :], wide(beta[:, a * 6:a * 6 + 6], P)))
            eng.sem_inc(gate_ok, 1)

            def conv(s):
                q = (gq, gk, gv)[s]
                eng.wait_ge(win_out, NTOK + 3 * s + 3)
                if s:
                    eng.wait_ge(silu_ok, s)
                for j in range(NH):
                    c = lambda i: pcol("conv", i * 18 + s * 6 + j)
                    done(ts(CACC[:, j, :], q[:, j, :], c(3), None, MUL))
                    for d in (1, 2, 3):
                        done(stt(CACC[:, j, d:T], q[:, j, 0:T - d], c(3 - d), CACC[:, j, d:T], MUL, ADD))
                eng.sem_inc(conv_in, 1)

            def squares(s):
                q = (gq, gk)[s]
                eng.wait_ge(silu_ok, s + 1)
                done(tt(CSQ, q, q, MUL))
                eng.sem_inc(conv_ok, 1)

            def unit(s):
                q = (gq, gk)[s]
                eng.wait_ge(gs_root, s + 1)
                done(v.reciprocal(CSQ, CSQ))
                done(stt(q, q, P ** -0.5 if s == 0 else 1.0, CSQ, MUL, MUL))
                eng.sem_inc(gn_ok, 1)

            conv(0)
            squares(0)
            eng.wait_ge(gate_mm, 1)
            done(v.tensor_copy(gcum, bank[6][:, 0:12]))
            for m in range(12):
                h, a = m // 2, m % 2
                done(ts(DT[:, m, :], bank[3 + m // 4][:, (m % 4) * P:(m % 4 + 1) * P], gcum[:, a * 6 + h:a * 6 + h + 1], 0.0, SUB, MIN))
            eng.sem_inc(gexp_in, 1)
            lg, dt = (q.rearrange("p a b -> p (a b)") for q in (LG, DT))
            conv(1)
            eng.wait_ge(gexp_ok, 1)
            done(tt(DT, DT, over(con("incl"), 12), MUL))
            eng.wait_ge(gate_mm, 2)
            for i in range(3):
                done(tt(lg[:, i * 512:(i + 1) * 512], bank[3 + i][:], dt[:, i * 512:(i + 1) * 512], MUL))
            done(tt(LG, LG, over(con("strict"), 12), MUL))
            done(v.tensor_copy(glast, EG[:, :, CH - 1:T:CH]))
            eng.sem_inc(gexp_ok, 1)
            unit(0)
            squares(1)
            conv(2)
            unit(1)

            for j in range(NJ):
                done(v.tensor_tensor_scan(T5[:, j, :], con("carry"), T3[:, j, :], 0.0, MUL, ADD))
            done(tt(T6, T5, T3, SUB))
            eng.sem_inc(cum_ok, 1)
            eng.wait_ge(silu_ok, 3)

            def shift_mix(i, diff):
                q = (pr, pk, pv, pg)[i]
                eng.wait_ge(win_out, NTOK + (12, 15, 18, 24)[i])
                done(tt(diff[:, :, 1:T], q[:, :, 0:T - 1], q[:, :, 1:T], SUB))
                done(ts(diff[:, :, 0:1], q[:, :, 0:1], -1.0, None, MUL))
                for j in range(NJ):
                    done(stt(q[:, j, :], diff[:, j, :], pcol("mu", i * NJ + j), q[:, j, :], MUL, ADD))

            for i in range(3):
                shift_mix(i, T1)
            for j in range(NJ):
                done(ts(T1[:, j, :], pk[:, j, :], pcol("k_k", j), None, MUL))
            done(tt(T2, T1, T1, MUL))
            eng.sem_inc(sq_ok, 1)
            eng.wait_ge(exp_ok, 2)
            done(v.reciprocal(T2, T2))
            done(tt(T1, T1, T2, MUL))
            done(tt(T2, T1, T4, MUL))
            done(tt(T2, T2, T3, MUL))
            for j in range(NJ):
                done(ts(T4[:, j, :], T4[:, j, :], -1.0, pcol("k_a", j), ADD, MUL))
            done(stt(pk, T4, 1.0, pk, ADD, MUL))
            for j in range(NJ):
                done(stt(T4[:, j, :], pr[:, j, :], pcol("r_k", j), pk[:, j, :], MUL, MUL))
            eng.sem_inc(bon_ok, 1)
            done(tt(T1, T1, T6, MUL))
            done(tt(pr, pr, T7, MUL))
            done(tt(pk, pk, T3, MUL))
            done(v.tensor_copy(elast, T7[:, :, CH - 1:T:CH]))
            for j in range(NJ):
                for src, dst in ((T2, T3), (pk, T5)):
                    done(tt(dst[:, j, :].rearrange("p (c t) -> p c t", c=NC), src[:, j, :].rearrange("p (c t) -> p c t", c=NC),
                            wide(elast[:, j, :], CH), MUL))
            for g in range(3):
                for i, dst in enumerate((dt, lg)):
                    p = 2 * g + i
                    eng.wait_ge(prod_mm, p + 1)
                    done(tt(dst[:, g * 512:(g + 1) * 512], bank[3 + p % 5][:], dst[:, g * 512:(g + 1) * 512], MUL))
                    eng.sem_inc(prod_ok, 1)
            done(tt(gq, gq, EG, MUL))
            shift_mix(3, view(0, NJ, T))
            eng.wait_ge(bon_mm, 1)
            t4, pvf = (q.rearrange("p a b -> p (a b)") for q in (T4, pv))
            for i in range(3):
                done(tt(t4[:, i * 512:(i + 1) * 512], bank[3 + i][:], pvf[:, i * 512:(i + 1) * 512], MUL))
            eng.sem_inc(bon_done, 1)
            eng.sem_inc(chan_ok, 1)

            done(tt(egc, egc, beta, MUL))
            kbe = tok(gk)
            for u in range(8, 12):
                a, b0 = u % 2, 2 * (u % 4)
                eng.wait_ge(tok_mm, 12 if u < 10 else u + 1)
                for h0, nh, bk in ((0, 4, b0), (4, 2, b0 + 1)):
                    ps = bank[bk][:, 0:nh * P].rearrange("p (h c) -> p h c", h=nh)
                    o = lambda t: t[:, a, h0 * P:(h0 + nh) * P].rearrange("p (h c) -> p h c", h=nh)
                    w = lambda t: wide(t[:, a * 6 + h0:a * 6 + h0 + nh], P)
                    if u < 10:
                        done(tt(o(kbe), ps, w(egc), MUL))
                        done(tt(o(KDG), ps, w(ekd), MUL))
                    else:
                        done(tt(o(VBG), ps, w(beta), MUL))
                eng.sem_inc(tok_d, 1)

            p = 6
            for bt in range(3):
                lt = LT3 if bt < 2 else LG.rearrange("p (g q) c -> p g (q c)", g=3)
                if bt < 2:
                    if bt:
                        eng.wait_ge(u1_mm, bt)
                        eng.wait_ge(lm_ok, 3 * (LEVELS - 1) * bt)
                    for g in range(3):
                        gg = bt * 3 + g
                        for dst, mask in ((LT3[:, g, :], "strict"), (LK3[:, g, :], "strict"), (RB[:, gg, :], "incl"), (RK[:, gg, :], "incl")):
                            eng.wait_ge(prod_mm, p + 1)
                            done(tt(dst.rearrange("p (q c) -> p q c", q=4), bank[p % 8][:].rearrange("p (q c) -> p q c", q=4),
                                    over(con(mask), 4), MUL))
                            eng.sem_inc(prod_ok, 1)
                            p += 1
                q4 = lambda t, g: t[:, g, :].rearrange("p (q c) -> p q c", q=4)
                if bt:
                    eng.wait_ge(u2_mm, bt)
                for g in range(3):
                    done(tt(q4(TI3, g), q4(lt, g), over(con("lev0"), 4), MUL))
                    done(tt(q4(TI3, g), over(con("ident"), 4), q4(TI3, g), SUB))
                eng.sem_inc(t0_ok, 1)
                for lv in range(1, LEVELS):
                    n = (bt * (LEVELS - 1) + lv - 1) * 3
                    for g in range(3):
                        eng.wait_ge(t_mm, n + g + 1)
                        if lv < LEVELS - 1:
                            done(tt(TM3[:, g, :], TM3[:, g, :], bank[2 * g + 1][:], SUB))
                        done(tt(TI3[:, g, :], TI3[:, g, :], bank[2 * g][:], SUB))
                        eng.sem_inc(t_ok, 1)

            eng.wait_ge(u2_ok, 3)
            done(v.memset(M1, 0.0))
            done(v.memset(S1, 0.0))
            eng.sem_inc(m_ok, 1)
            for c in range(NC):
                a, base = c // 2, CH * (c % 2)
                rows = slice(base, base + CH)
                eng.wait_ge(su_mm, c + 1)
                for b0, u0, u in ((0, tok(pv), tok(T2)), (2, tok(gv), VBG)):
                    done(tt(u[rows, a, 0:512], u0[rows, a, 0:512], bank[b0][rows, :], SUB))
                    done(tt(u[rows, a, 512:768], u0[rows, a, 512:768], bank[b0 + 1][rows, 0:256], SUB))
                eng.sem_inc(su_ok, 1)
                if c == NC - 1:
                    break
                eng.wait_ge(sx_mm, c + 1)
                done(tt(M1, M1, wide(elast[:, :, c], P), MUL))
                done(tt(S1, S1, wide(glast[:, :, c], P), MUL))
                eng.wait_ge(sm_mm, c + 1)
                for j0, nj, bk in ((0, 4, 0), (4, 2, 1)):
                    done(tt(MTMP[:, j0:j0 + nj, :], bank[bk][:, 0:nj * P].rearrange("p (j c) -> p j c", j=nj), over(con("bd"), nj), MUL))
                done(tt(M1, M1, MTMP, ADD))
                for j0, nj, bk in ((0, 4, 2), (4, 2, 3)):
                    done(tt(S1[:, j0:j0 + nj, :], S1[:, j0:j0 + nj, :], bank[bk][:, 0:nj * P].rearrange("p (j c) -> p j c", j=nj), ADD))
                eng.sem_inc(m_ok, 1)

            eng.wait_ge(so_ok, TT)
            n3 = lambda t, w: t.rearrange("p a (h c) -> p a h c", c=w).rearrange("p a h c -> p (a h) c")
            nt = lambda g: NTMP.rearrange("p (g c) -> p g c", g=g)
            o64 = pk.rearrange("p a b -> p (a b)").rearrange("p (g c) -> p g c", c=CH)
            head_norm(3, o64, nt(24), 24, CH, stat2, True, 64e-5)
            eng.sem_inc(o_ok, 1)
            og = OG.rearrange("p a b -> p (a b)").rearrange("p (g c) -> p g c", c=P)
            head_norm(4, og, nt(12), 12, P, stat[:, 0:12], False, 1e-6)
            eng.sem_inc(o_ok, 1)
            eng.wait_ge(gates_ok, 1)
            eng.wait_ge(mt_mm, 1)
            for j in range(NJ):
                done(ts(MIX[:, j, :], bank[j // 2][:, (j % 2) * T:(j % 2 + 1) * T], pcol("ln_w", j), pcol("ln_b", j), MUL, ADD))
            done(tt(MIX[:, 0:NJ], MIX[:, 0:NJ], T4, ADD))
            done(tt(MIX[:, 0:NJ], MIX[:, 0:NJ], pg, MUL))
            eng.sem_inc(mt_ok, 1)
            eng.wait_ge(mt_mm, 2)
            for j in range(NH):
                done(stt(MIX[:, NJ + RH + j, :], bank[3 + j // 2][:, (j % 2) * T:(j % 2 + 1) * T], pcol("gdn_w", j), gz[:, j, :], MUL, MUL))
            eng.sem_inc(mt_ok, 1)
            eng.wait_ge(mt_mm, 3)
            for j in range(RH):
                done(stt(MIX[:, NJ + j, :], bank[6 + j // 2][:, (j % 2) * T:(j % 2 + 1) * T], pcol("gn_w", j), rg[:, j, :], MUL, MUL))
            eng.sem_inc(mt_ok, 1)

            eng.wait_ge(x2_in, 16)
            eng.wait_ge(wo_mm, K)
            for a in range(TT):
                for n in range(4):
                    done(tt(X[:, a, n * 512:(n + 1) * 512], X[:, a, n * 512:(n + 1) * 512], bank[a * 4 + n][:], ADD))
            rms(5, X, lambda a: XS[:, a])
            for a in range(TT):
                done(ts(XS[:, a], X[:, a], rstd[:, a:a + 1], None, MUL))
            eng.sem_inc(xs_ok, 1)
            for r in range(8):
                eng.wait_ge(xs_mm, r + 1)
                for kk in range(2):
                    k = 2 * r + kk
                    done(ts(XTT[:, k, :], bank[r % 4][:, kk * T:(kk + 1) * T], pcol("norm2", k), None, MUL))
                eng.sem_inc(xs_t, 1)
            eng.wait_ge(lg_mm, 1)
            for a in range(TT):
                done(tt(LGT[:, a, :], bank[4 + a][:, 0:36], pcol("router_b", 0, 36), ADD))
            gl, el = LGT[:, :, 0:4], LGT[:, :, 4:36]
            s = lambda i: stat[:, 2 * i:2 * i + 2]
            s2 = lambda i: stat2[:, 2 * i:2 * i + 2]
            iota = con("iota")

            def first_max(vals, n, top, tmp, onehot):
                done(v.tensor_reduce(top, vals, AX, MAX))
                done(tt(tmp, vals, wide(top, n), EQ))
                done(ts(tmp, tmp, -99.0, 99.0, MUL, ADD))
                done(tt(tmp, tmp, over(iota[:, 0:n], TT), ADD))
                done(v.tensor_reduce(s2(5), tmp, AX, MIN))
                done(tt(onehot, over(iota[:, 0:n], TT), wide(s2(5), n), EQ))

            first_max(gl, 4, s(0), R6[:, :, 0:4], R3[:, :, 0:4])
            done(tt(R1[:, :, 0:4], gl, wide(s(0), 4), SUB))
            eng.sem_inc(rex_in, 1)
            eng.wait_ge(rex_ok, 1)
            done(v.tensor_reduce(s(1), R2[:, :, 0:4], AX, ADD))
            done(v.reciprocal(s(1), s(1)))
            for a in range(TT):
                done(v.tensor_copy(R4[:, a].rearrange("p (g e) -> p g e", g=4), wide(R3[:, a, 0:4], 8)))
            done(tt(R5, el, R4, MUL))
            done(ts(R4, R4, 1e30, -1e30, MUL, ADD))
            done(tt(R5, R5, R4, ADD))
            first_max(R5, NE, s(2), R6, R3)
            done(stt(R5, R3, -2e30, R5, MUL, ADD))
            first_max(R5, NE, s(3), R6, R4)
            done(tt(s2(0), s(3), s(2), SUB))
            eng.sem_inc(rex_in, 1)
            eng.wait_ge(rex_ok, 2)
            done(ts(s2(1), s2(0), 1.0, None, ADD))
            done(v.reciprocal(s2(1), s2(1)))
            done(tt(s2(1), s2(1), s(1), MUL))
            done(tt(s2(0), s2(0), s2(1), MUL))
            done(tt(R1, R3, R4, ADD))
            eng.sem_inc(e_ok, 1)
            done(tt(R3, R3, wide(s2(1), NE), MUL))
            done(tt(R4, R4, wide(s2(0), NE), MUL))
            done(tt(GE, R3, R4, ADD))
            eng.wait_ge(pos_mm, 1)
            done(stt(posm, bank[6][:, 0:64].rearrange("p (a e) -> p a e", a=TT), 1.0, R1, ADD, MUL))
            done(ts(posm, posm, -1.0, None, ADD))
            done(v.tensor_reduce(s(4)[:, 0:1], bank[6][:, 64:96], AX, MAX))
            done(ts(flag[:], s(4)[:, 0:1], float(TOPC), None, ALU.is_gt))
            eng.sem_inc(flag_ok, 1)

            def experts(r, first):
                st = lambda n: n
                for a in range(TT):
                    one(tt(PS[:, a].rearrange("p (e s) -> p e s", e=NE), over(iota, NE), wide(posm[:, a], TOPC), EQ), r, 0 + 2 * a)
                    one(tt(PG[:, a].rearrange("p (e s) -> p e s", e=NE), PS[:, a].rearrange("p (e s) -> p e s", e=NE),
                           wide(GE[:, a], TOPC), MUL), r, 1 + 2 * a)
                one(ts(posm, posm, -float(TOPC), None, ADD), r, 4)
                if not first:
                    eng.sem_inc(pass_go, 1)
                    eng.wait_ge(xs_in, r * 16)
                eng.sem_inc(p_ok, 1)
                for k in range(K):
                    eng.wait_ge(g_mm, r * 32 + (2 * k + 2))
                    if k == K - 1:
                        eng.wait_ge(g_act, r * K + K)
                        eng.wait_ge(sg_ok, r * 4 + 4)
                    ts(XT[:, k, 512:1024], bank[4 + (2 * k + 1) % 4][:], pcol("norm2", k), None, MUL).then_inc(g_dve, 1)
                with eng.Fori(0, 8) as i:
                    def stage(b):
                        if b == 0:
                            eng.wait_ge(g_dve, r * K + K)
                        if b >= 2:
                            eng.wait_ge(up_mm, r * NE + i * 4 + (b - 1))
                        v.tensor_copy(XE[b % 2], XT[:, :, bass.ds(i * P + b * TOPC, TOPC)]).then_inc(xe_ok, 1)

                    def hid(b):
                        eng.wait_ge(gs_ok, r * NE + i * 4 + (b + 1))
                        if b >= 2:
                            eng.wait_ge(dn_mm, r * NE + i * 4 + (b - 1))
                        tt(HD[b % 2].rearrange("p f s -> p (f s)"), GS, bank[2][:, 64:128], MUL).then_inc(hd_ok, 1)

                    v.tensor_copy(SGQ, SG.rearrange("p a b -> p (a b)")[:, bass.ds(i * T, T)]).then_inc(sgq_ok, 1)
                    stage(0)
                    stage(1)
                    stage(2)
                    hid(0)
                    stage(3)
                    hid(1)
                    hid(2)
                    hid(3)
                    eng.wait_ge(dn_mm, r * NE + i * 4 + 4)
                    v.tensor_copy(YS[:, 1024:1536], bank[5][:]).then_inc(yd_half, 1)
                    v.tensor_copy(YS[:, 1536:2048], bank[6][:]).then_inc(yd_half, 1)
                    eng.wait_ge(yd_half, r * 16 + i * 2 + 2)
                    eng.sem_inc(yd_ok, 1)
                    for q in range(8):
                        a, n = q // 4, q % 4
                        eng.wait_ge(sc_mm, (r * 8 + i) * 8 + (q + 1))
                        c = slice(n * 512, (n + 1) * 512)
                        tt(X[:, a, c], X[:, a, c], bank[7 if q % 2 else 2][:], ADD).then_inc(sc_ok, 1)
                    eng.wait_ge(sc_ok, (r * 8 + i) * 8 + 8)

            def one(ins, r, n):
                ins.then_inc(p_step, 1)
                eng.wait_ge(p_step, r * 5 + (n + 1))

            experts(0, True)
            with eng.If(eng.value_load(flag[0:1, 0:1]) == 1):
                with eng.Fori(1, PASSES) as r:
                    experts(r, False)
            eng.sem_inc(fin_go, 1)
            rms(6, X, lambda a: JUNK)
            eng.wait_ge(fw_in, 16)
            for a in range(TT):
                stt(X[:, a], X[:, a], rstd[:, a:a + 1], FW, MUL, MUL).then_inc(y_ok, 1)


class Steps:

    def __init__(self, eng, sem):
        self.eng, self.sem, self.n = eng, sem, 0

    def __call__(self, ins):
        self.n += 1
        ins.then_inc(self.sem, 1)
        self.eng.wait_ge(self.sem, self.n)


def kernel(**inputs):
    import concourse.bacc as bacc
    from concourse.bass_utils import run_bass_kernel_spmd

    a = {n: np.ascontiguousarray(v) for n, v in inputs.items()}

    def rows(v):
        return v.reshape(-1, P).T

    def alike(v):
        return np.broadcast_to(v.reshape(1, -1), (P, v.size))

    par = np.concatenate([rows(a["rwkv_mu_rkvg"]), rows(a["rwkv_w0"]), rows(a["rwkv_a0"]), rows(a["rwkv_k_k"]), rows(a["rwkv_k_a"]),
                          rows(a["rwkv_r_k"]), rows(a["rwkv_ln_w"]), rows(a["rwkv_ln_b"]), rows(a["ret_gn_w"]), rows(a["gdn_norm_w"]),
                          rows(a["gdn_conv_w"]), a["norm1_w"].reshape(P, K), a["rwkv_mu_wa"][0, 0].reshape(P, K),
                          a["rwkv_mu_wa"][0, 1].reshape(P, K), a["norm2_w"].reshape(P, K), alike(a["gdn_dt_bias"]),
                          alike(a["gdn_a_log"]), alike(a["moe_group_b"]), alike(a["moe_expert_b"])], axis=1)
    feeds = {
        "x": a["x"].reshape(T, D),
        "positions": np.ascontiguousarray(a["positions"].reshape(TT, P).T),
        "w_in": a["w_in"].reshape(D, N_IN),
        "w_out": a["w_out"].reshape(D, D),
        "lora1": np.stack([a["rwkv_w1"][0], a["rwkv_a1"][0]]),
        "lora2": np.stack([a["rwkv_w2"][0], a["rwkv_a2"][0]], axis=1),
        "par": np.ascontiguousarray(par),
        "consts": np.concatenate(list(const_arrays().values()), axis=1),
        "router": np.concatenate([a["moe_group_w"][0], a["moe_expert_w"][0]], axis=1),
        "w1": a["moe_w1"].reshape(NE, D, HID),
        "w3": a["moe_w3"].reshape(NE, D, HID),
        "w2": a["moe_w2"].reshape(NE, HID, D),
        "final_w": np.ascontiguousarray(alike(a["final_norm_w"])),
    }
    nc = bacc.Bacc("TRN2", target_bir_lowering=False, num_devices=1)
    aps = [nc.dram_tensor(n, v.shape, mybir.dt.from_np(v.dtype), kind="ExternalInput").ap() for n, v in feeds.items()]
    scratch = nc.dram_tensor("xt_scratch", (T, D), F32, kind="Internal").ap()
    out = nc.dram_tensor("out", (T, D), F32, kind="ExternalOutput").ap()
    trunk(nc, *aps, scratch, out)
    return run_bass_kernel_spmd(nc, [feeds], core_ids=[0]).results[0]["out"].reshape(1, T, D)
```

```python
from contextlib import ExitStack

import numpy as np

import concourse.bass as bass
from concourse import mybir

F32 = mybir.dt.float32
I32 = mybir.dt.int32
ALU = mybir.AluOpType
ACT = mybir.ActivationFunctionType
AX = mybir.AxisListType.X

P = 128
D = 2048
T = 256
TT = T // P
K = D // P
RW, RT, GD = 768, 512, 768
NJ = RW // P
NH = GD // P
RH = RT // P
N_IN = 4 * RW + 4 * RT + 4 * GD + 2 * NH
CH = 64
NC = T // CH
DECAY = 0.6065306597126334
NE, TOPC, HID = 32, 32, 256
PASSES = T // TOPC
CW = 256
NTOK = 3 * RT // CW
COL_RWKV, COL_RET, COL_RETG, COL_GDN, COL_AB = 0, 4 * RW, 4 * RW + 3 * RT, 4 * RW + 4 * RT, N_IN - 2 * NH
PI_LO = 3.1415925
LEVELS = 6


SEGMENTS = [(24, COL_GDN), (30, COL_GDN + GD), (36, COL_GDN + 2 * GD), (0, COL_RWKV), (6, COL_RWKV + RW),
            (12, COL_RWKV + 2 * RW), (42, COL_GDN + 3 * GD), (18, COL_RWKV + 3 * RW), (48, COL_RETG)]
NCHUNK = NTOK + 26
ORDER = list(range(NJ, NJ + RH)) + list(range(NJ)) + list(range(NJ + RH, K))


def param_columns():
    at, col = 0, {}
    for name, n in (("mu", 4 * NJ), ("w0", NJ), ("a0", NJ), ("k_k", NJ), ("k_a", NJ), ("r_k", NJ), ("ln_w", NJ),
                    ("ln_b", NJ), ("gn_w", RH), ("gdn_w", NH), ("conv", 4 * 3 * NH), ("norm1", K), ("mu_w", K),
                    ("mu_a", K), ("norm2", K), ("dt", NH), ("alog", NH), ("router_b", 36)):
        col[name] = at
        at += n
    return col, at


def const_arrays():
    s, t = np.arange(P)[:, None], np.arange(P)[None, :]
    same = (s // CH) == (t // CH)
    lg = np.log(1.0 - 2.0 ** (-5.0 - np.arange(RH)))
    out = {"ident": s == t,
           "stack": (s % TOPC) == np.arange(TOPC)[None, :],
           "iota": np.broadcast_to(np.arange(NE)[None, :], (P, NE)),
           "bd": same,
           "incl": same & (s <= t),
           "strict": same & (s < t),
           "after": same & (s > t),
           "ones": np.ones((P, P)),
           "before": s < t}
    for lv in range(LEVELS):
        b = 2 ** lv
        out[f"lev{lv}"] = ((s // b) % 2 == 0) & (t // b == s // b + 1)
    out["carry"] = np.broadcast_to(np.arange(T)[None, :] % CH != 0, (P, T))
    out["dmask"] = np.concatenate([np.where(s <= t, np.exp(np.maximum(t - s, 0) * g), 0.0) for g in lg], 1) * P ** -0.5
    out["qdec"] = np.exp((s + 1.0) * lg[None, :])
    out["kdec"] = np.exp((P - 1.0 - s) * lg[None, :]) * P ** -0.5
    out["freq"] = np.broadcast_to((np.float32(10000.0) ** (-np.arange(0, P, 2, dtype=np.float32) / P))[None, :], (P, 64))
    return {n: np.ascontiguousarray(a, dtype=np.float32) for n, a in out.items()}


def trunk(nc, x, positions, w_in, w_out, lora1, lora2, par, consts, router, w1, w3, w2, final_w, out):
    col, npar = param_columns()
    ccol, at = {}, 0
    for name, a in const_arrays().items():
        ccol[name] = (at, a.shape[1])
        at += a.shape[1]
    ncon = at

    with ExitStack() as ctx:
        def sem(name):
            return ctx.enter_context(nc.semaphore(name))

        mem = ctx.enter_context(nc.sbuf_tensor("mem", [P, 204 * 256], F32))
        prm = ctx.enter_context(nc.sbuf_tensor("prm", [P, npar], F32))
        small = ctx.enter_context(nc.sbuf_tensor("small", [P, 320], F32))
        posi = ctx.enter_context(nc.sbuf_tensor("posi", [P, TT], I32))
        flag = ctx.enter_context(nc.sbuf_tensor("flag", [P, 1], I32))
        bank = [ctx.enter_context(nc.psum_tensor(f"bank{i}", [P, 512], F32)) for i in range(8)]

        def view(kb, *shape):
            n = int(np.prod(shape))
            assert kb * 256 + n <= 204 * 256
            v = mem[:, int(kb * 256):int(kb * 256) + n]
            if len(shape) == 2:
                v = v.rearrange("p (a b) -> p a b", a=shape[0])
            elif len(shape) == 3:
                v = v.rearrange("p (a b c) -> p a b c", a=shape[0], b=shape[1])
            return v

        def con(name):
            a, n = ccol[name]
            return view(187, ncon)[:, a:a + n]

        def pcol(name, j, n=1):
            return prm[:, col[name] + j:col[name] + j + n]

        def over(ap, n):
            return ap.unsqueeze(1).broadcast_to([P, n, ap.shape[-1]])

        def tok(v):
            return v.rearrange("p a b -> p (a b)").rearrange("p (a c) -> p a c", a=TT)

        def wide(ap, n):
            return ap.unsqueeze(2).broadcast_to([P, ap.shape[-1], n])

        X = view(0, TT, D)
        PJ = view(16, 52, T)
        pr, pk, pv, pg = (PJ[:, NJ * i:NJ * i + NJ, :] for i in range(4))
        gq, gk, gv, gz = (PJ[:, 24 + NH * i:24 + NH * i + NH, :] for i in range(4))
        rg = PJ[:, 48:52, :]
        XW, XA, XN = view(16, K, T), view(32, K, T), view(48, TT, D)
        DH = view(48, K, T)
        TM = view(68, TT, 3 * RT)
        AB = small[:, 0:24].rearrange("p (a b) -> p a b", a=TT)
        HT = view(81, K, T)
        RING = [view(97 + 16 * b, K, CW) for b in range(3)]
        T1, T2, T3, T4, T5, T6, T7 = (view(145 + 6 * i, NJ, T) for i in range(7))
        L1 = view(145, 2, K, 96)
        L2 = view(169, 2, RW)
        WAB = view(200, K, 12)
        LH = view(201, 2, T)
        COS, SIN, ANG, ANR = (view(v, TT, 64) for v in (10, 10.5, 11, 11.5))
        QR, KR = view(175, TT, RT), view(181, TT, RT)
        QT, KT = view(0, TT, RH, P), view(12, TT, RH, P)
        KD0 = view(4, RT)
        ST = view(181, TT, RH, P)
        KV0 = view(175, RT)
        RTMP = view(198, RT)
        YR = view(6, TT * RH, P)
        YQ = view(198, 2 * RH, P)
        LT3, TM3, TI3, AS3, LK3 = (view(81 + 6 * i, 3, 512) for i in range(5))
        RB, RK = view(111, 6, 512), view(123, 6, 512)
        LM3 = view(135, 3, 512)
        EG, DT, LG = view(68, NH, T), view(74, NH * TT, P), view(198, NH * TT, P)
        KDG, VBG, WTG = view(68, TT, GD), view(0, TT, GD), view(10, NH, T)
        GTMP1, GTMP2 = view(175, 12, P), view(181, 12, P)
        CACC, CSQ = T1, T2
        X1 = view(99, 3, 256)
        M1, S1, MTMP = view(81, NJ, P), view(84, NH, P), view(87, NJ, P)
        OG = view(105, TT, GD)
        NTMP = view(87, TT * GD)
        MIX = view(113, K, T)
        WO = [view(v, D) for v in (40, 48, 68, 177, 16, 24)]
        XS = view(16, TT, D)
        XTT = view(56, K, T)
        RWT = view(198, K, 36)
        PS, PG = view(32, TT, NE * TOPC), view(40, TT, NE * TOPC)
        SG = view(48, 8, T)
        XQ, XN4 = (view(v, K, 4 * TOPC) for v in (56, 64))
        YS = view(72, D)
        WU = [view(81 + 48 * b, 2, K, HID) for b in range(2)]
        WD = [view(81 + 48 * b + 32, 2, D) for b in range(2)]
        UP = [view(177 + 2 * b, 512) for b in range(2)]
        GS = view(185, 64)
        HD = [view(185.25 + 0.25 * b, 2, TOPC) for b in range(2)]
        SGQ = view(185.75, T)
        FW = view(188, D)
        JUNK = view(81, D)

        tiny = iter(range(24, 320))

        def cols(n):
            a = [next(tiny) for _ in range(n)]
            return small[:, a[0]:a[0] + n]

        ssq, rstd = cols(2), cols(2)
        elast = cols(24).rearrange("p (a b) -> p a b", a=NJ)
        glast = cols(24).rearrange("p (a b) -> p a b", a=NH)
        beta, gate, egc, ekd = cols(12), cols(12), cols(12), cols(12)
        gcum = cols(12)
        posf, stat, stat2 = cols(2), cols(24), cols(24)
        ea, eps6 = cols(6), cols(1)
        posm = cols(64).rearrange("p (a b) -> p a b", a=TT)
        LGT = view(179, TT, 36)
        R1, R2, R3, R4, R5, R6 = (view(179.5 + 0.25 * i, TT, NE) for i in range(6))
        GE = view(186.75, TT, NE)

        x_in = [sem(f"x_in{a}") for a in range(TT)]
        c_in, tables_in, lora_in, ab_in = sem("c_in"), sem("tables_in"), sem("lora_in"), sem("ab_in")
        win_in = [sem(f"win_in{b}") for b in range(3)]
        win_mm, win_out = sem("win_mm"), sem("win_out")
        dve, act = sem("dve"), sem("act")
        ss_ok, std_ok = sem("ss_ok"), sem("std_ok")
        ss_mm = sem("ss_mm")
        xn_ok, xt_mm, ht_ok = sem("xn_ok"), sem("xt_mm"), sem("ht_ok")
        xwa_ok, lo_mm, lo_ok, lo2_mm, sig_ok = sem("xwa_ok"), sem("lo_mm"), sem("lo_ok"), sem("lo2_mm"), sem("sig_ok")
        ang_ok, sin_ok, ab_mm, ab_ok = sem("ang_ok"), sem("sin_ok"), sem("ab_mm"), sem("ab_ok")
        rot_ok, rt_mm, rt_ok, ry_ok = sem("rot_ok"), sem("rt_mm"), sem("rt_ok"), sem("ry_ok")
        cum_ok, exp_ok, sq_ok, sq_mm = sem("cum_ok"), sem("exp_ok"), sem("sq_ok"), sem("sq_mm")
        bon_ok, bon_mm, bon_done, chan_ok = sem("bon_ok"), sem("bon_mm"), sem("bon_done"), sem("chan_ok")
        tok_mm, tok_ok = sem("tok_mm"), sem("tok_ok")
        conv_ok, silu_ok, gn_ok = sem("conv_ok"), sem("silu_ok"), sem("gn_ok")
        ga_ok, gb_ok, gate_ok, gate_mm, gexp_in, gexp_ok = (sem(n) for n in (
            "ga_ok", "gb_ok", "gate_ok", "gate_mm", "gexp_in", "gexp_ok"))
        prod_mm, prod_ok = sem("prod_mm"), sem("prod_ok")
        t0_ok, t0_mm, t0_sb = sem("t0_ok"), sem("t0_mm"), sem("t0_sb")
        lm_ok, a_mm, a_sb, t_mm, t_ok = sem("lm_ok"), sem("a_mm"), sem("a_sb"), sem("t_mm"), sem("t_ok")
        u1_mm, u1_ok, u2_mm, u2_ok = sem("u1_mm"), sem("u1_ok"), sem("u2_mm"), sem("u2_ok")
        m_ok, su_mm, su_ok, sm_mm, so_mm, so_ok = (sem(n) for n in ("m_ok", "su_mm", "su_ok", "sm_mm", "so_mm", "so_ok"))
        o_ok, mt_mm, mt_ok = sem("o_ok"), sem("mt_mm"), sem("mt_ok")
        x2_in, wo_mm, wo_tile = sem("x2_in"), sem("wo_mm"), sem("wo_tile")
        wo_in = [sem(f"wo_in{b}") for b in range(6)]
        x1_ok, xs_ok, xs_mm, xs_t, rw_in, lg_mm, rex_in, rex_ok = (sem(n) for n in (
            "x1_ok", "xs_ok", "xs_mm", "xs_t", "rw_in", "lg_mm", "rex_in", "rex_ok"))
        e_ok, pos_mm, flag_ok, xs_out, xs_in = sem("e_ok"), sem("pos_mm"), sem("flag_ok"), sem("xs_out"), sem("xs_in")
        p_ok, sg_mm, sg_ok, g_mm, g_act, g_dve = (sem(n) for n in ("p_ok", "sg_mm", "sg_ok", "g_mm", "g_act", "g_dve"))
        wu_in = [sem(f"wu_in{b}") for b in range(2)]
        wd_in = [sem(f"wd_in{b}") for b in range(2)]
        xe_ok, up_mm, up_sb, h_mm, gs_ok, hd_ok, dn_mm = (sem(n) for n in (
            "xe_ok", "up_mm", "up_sb", "h_mm", "gs_ok", "hd_ok", "dn_mm"))
        ya_ok, yd_ok, sc_mm, sc_ok, sq_stage = (sem(n) for n in ("ya_ok", "yd_ok", "sc_mm", "sc_ok", "sq_stage"))
        wu_free = [sem(f"wu_free{b}") for b in range(2)]
        wd_free = [sem(f"wd_free{b}") for b in range(2)]
        tok_a, tok_d, rt_dve, sx_mm, pass_go, fin_go, sgq_ok = (sem(n) for n in (
            "tok_a", "tok_d", "rt_dve", "sx_mm", "pass_go", "fin_go", "sgq_ok"))
        conv_in, gs_root, gates_ok, ya_half, yd_half, p_step, xs_stored = (sem(n) for n in (
            "conv_in", "gs_root", "gates_ok", "ya_half", "yd_half", "p_step", "xs_stored"))
        pg_mixed = sem("pg_mixed")
        fw_in, y_ok, out_done = sem("fw_in"), sem("y_ok"), sem("out_done")
        g_ok, g_part, xq_ok, pg_ok = sem("g_ok"), sem("g_part"), sem("xq_ok"), sem("pg_ok")

        def product_bank(p):
            return (p - 6) % 8 if p < 18 else (p + 5) % 8

        wv = w_in.rearrange("(p k) n -> p k n", k=K)
        w1v = w1.rearrange("e (p k) f -> p e (k f)", k=K)
        w3v = w3.rearrange("e (p k) f -> p e (k f)", k=K)
        w2v = w2.rearrange("e (f p) n -> p e f n", p=P)
        xv = x.rearrange("(a p) n -> p a n", p=P)
        ov = out.rearrange("(a p) n -> p a n", p=P)
        wov = w_out.rearrange("(k p) n -> p k n", p=P)

        block = ctx.enter_context(nc.Block())

        @block.sync
        def _(sp):
            for a in range(TT):
                sp.dma_start(X[:, a], xv[:, a]).then_inc(x_in[a], 16)
            sp.dma_start(con("ident"), consts[:, 0:P]).then_inc(c_in, 16)
            sp.dma_start(prm[:], par).then_inc(c_in, 16)

            def load(n, b, c0):
                sp.dma_start(RING[b], wv[:, :, c0]).then_inc(win_in[b], 16)

            for n in range(NTOK):
                if n >= 3:
                    sp.wait_ge(win_mm, n - 2)
                load(n, n % 3, slice(COL_RET + n * CW, COL_RET + (n + 1) * CW))
                if n == 0:
                    sp.dma_start(view(187, ncon)[:, P:ncon], consts[:, P:ncon]).then_inc(tables_in, 16)
                    sp.dma_start(posi[:], positions).then_inc(tables_in, 16)
                if n == 2:
                    sp.dma_start(WAB, wv[:, :, COL_AB:N_IN]).then_inc(ab_in, 16)
                    sp.dma_start(L1, lora1.rearrange("a (p k) r -> p a k r", k=K)).then_inc(lora_in, 16)
                    sp.dma_start(L2[0:96], lora2).then_inc(lora_in, 16)
            for first, c_from in ((NTOK, COL_GDN), (NTOK + 9, COL_RWKV)):
                with sp.Fori(0, 3) as i:
                    for b in range(3):
                        sp.wait_ge(win_mm, i * 3 + (first + b - 2))
                        load(None, b, bass.ds(i * (3 * CW) + (c_from + b * CW), CW))
            for n in range(NTOK + 18, NCHUNK):
                c0 = SEGMENTS[(n - NTOK) // 3][1] + (n - NTOK) % 3 * CW
                sp.wait_ge(win_mm, n - 2)
                load(n, n % 3, slice(c0, c0 + CW))
            sp.wait_ge(so_mm, TT)
            def load_up(e, s):
                for w, src in enumerate((w1v, w3v)):
                    sp.dma_start(WU[s][:, w].rearrange("p k f -> p (k f)").unsqueeze(1), src[:, e, :]).then_inc(wu_in[s], 16)

            def load_down(e, s):
                sp.dma_start(WD[s].unsqueeze(1), w2v[:, e, :, :]).then_inc(wd_in[s], 16)

            for k in range(K):
                if k >= 6:
                    sp.wait_ge(wo_mm, k - 5)
                if k == 4:
                    sp.wait_ge(mt_mm, 2)
                sp.dma_start(WO[k % 6], wov[:, ORDER[k], :]).then_inc(wo_in[k % 6], 16)
                if k == 5:
                    sp.dma_start(X, xv).then_inc(x2_in, 16)
                elif k == 7:
                    sp.wait_ge(mt_ok, 3)
                    load_up(slice(0, 1), 0)
                elif k == 10:
                    load_up(slice(1, 2), 1)
                elif k == 13:
                    load_down(slice(1, 2), 1)
                elif k == 14:
                    sp.dma_start(RWT, router.rearrange("(p k) n -> p k n", k=K)).then_inc(rw_in, 16)
            sp.wait_ge(wo_tile, 2)
            load_down(slice(0, 1), 0)

            def later_experts(r):
                def load(b, use, e):
                    s = b % 2
                    sp.wait_ge(wu_free[s], use)
                    load_up(e, s)
                    sp.wait_ge(wd_free[s], use)
                    load_down(e, s)

                with sp.Fori(0, 7) as i:
                    for b in range(4):
                        load(b, r * 16 + i * 2 + (b // 2 + 1), bass.ds(i * 4 + (b + 2), 1))
                for b in range(2):
                    load(b, r * 16 + 15, slice(30 + b, 31 + b))

            later_experts(0)
            sp.dma_start(FW, final_w).then_inc(fw_in, 16)
            sp.wait_ge(flag_ok, 1)
            with sp.If(sp.value_load(flag[0:1, 0:1]) == 1):
                with sp.Fori(1, PASSES) as r:
                    for b in range(2):
                        sp.wait_ge(wu_free[b], r * 16)
                        load_up(slice(b, b + 1), b)
                        sp.wait_ge(wd_free[b], r * 16)
                        load_down(slice(b, b + 1), b)
                    later_experts(r)
            for a in range(TT):
                sp.wait_ge(y_ok, a + 1)
                sp.dma_start(ov[:, a], X[:, a]).then_inc(out_done, 16)
            sp.wait_ge(out_done, 16 * TT)

        @block.gpsimd
        def _(pool):
            for bt in range(3):
                for lv in range(1, LEVELS):
                    n = (bt * (LEVELS - 1) + lv - 1) * 3
                    for g in range(3):
                        pool.wait_ge(prod_ok, 7 + bt * 12 + g * 4 if bt < 2 else 6)
                        if n:
                            pool.wait_ge(a_mm, n - 3 + g + 1)
                        src = LT3[:, g, :].rearrange("p (q c) -> p q c", q=4) if bt < 2 else LG[:, 4 * g:4 * g + 4, :]
                        nc.gpsimd.tensor_tensor(LM3[:, g, :].rearrange("p (q c) -> p q c", q=4), src,
                                                over(con(f"lev{lv}"), 4), ALU.mult).then_inc(lm_ok, 1)

        @block.tensor
        def _(pe):
            mm = nc.tensor.matmul
            ident, stack = con("ident"), con("stack")

            pe.wait_ge(c_in, 32)
            pe.wait_ge(xn_ok, 1)
            xn = XN.rearrange("p a (d k) -> p a k d", k=K)
            for r in range(8):
                if r >= 4:
                    pe.wait_ge(ht_ok, r - 3)
                for kk in range(2):
                    for a in range(TT):
                        o = kk * T + a * P
                        last = nc.tensor.transpose(bank[3 + r % 4][:, o:o + P], xn[:, a, 2 * r + kk, :], ident)
                last.then_inc(xt_mm, 1)
            pe.wait_ge(ht_ok, 8)

            def win_token(b):
                for a in range(TT):
                    for k in range(K):
                        last = mm(bank[b][:, a * CW:(a + 1) * CW], HT[:, k, a * P:(a + 1) * P], RING[b][:, k, :],
                                  start=(k == 0), stop=(k == K - 1), skip_group_check=True)
                last.then_inc(win_mm, 1)

            def win_chan(b):
                for c in range(2):
                    for k in range(K):
                        last = mm(bank[b][:, c * T:(c + 1) * T], RING[b][:, k, c * P:(c + 1) * P], HT[:, k, :],
                                  start=(k == 0), stop=(k == K - 1), skip_group_check=True)
                last.then_inc(win_mm, 1)

            def channel_sums(weights, src, banks):
                flat = src.rearrange("p a b -> p (a b)")
                for i, bk in enumerate(banks):
                    last = mm(bank[bk][:], weights, flat[:, i * 512:(i + 1) * 512], start=True, stop=True)
                return last

            def product(p, bk, f):
                for q in range(4):
                    lhs, rhs = f(q)
                    last = mm(bank[bk][:, q * P:(q + 1) * P], lhs, rhs, start=True, stop=True, skip_group_check=True)
                last.then_inc(prod_mm, 1)

            def low_rank_and_ab():
                pe.wait_ge(tables_in, 32)
                pe.wait_ge(ab_in, 16)
                for a in range(TT):
                    for k in range(K):
                        last = mm(bank[3][:, a * 12:(a + 1) * 12], HT[:, k, a * P:(a + 1) * P], WAB[:, k, :],
                                  start=(k == 0), stop=(k == K - 1), skip_group_check=True)
                last.then_inc(ab_mm, 1)
                pe.wait_ge(lora_in, 32)
                pe.wait_ge(xwa_ok, 1)
                for f, src in enumerate((XW, XA)):
                    for k in range(K):
                        last = mm(bank[4][0:96, f * T:(f + 1) * T], L1[:, f, k, :], src[:, k, :],
                                  start=(k == 0), stop=(k == K - 1), skip_group_check=True)
                last.then_inc(lo_mm, 1)

            def low_rank_out(f):
                if f:
                    pe.wait_ge(sig_ok, 1)
                else:
                    pe.wait_ge(rt_ok, 1)
                for half in range(3):
                    for jj in range(2):
                        j = half * 2 + jj
                        last = mm(bank[5 + half][:, jj * T:(jj + 1) * T], L2[0:96, f, j * P:(j + 1) * P], LH[0:96, f, :],
                                  start=True, stop=True, skip_group_check=True)
                    last.then_inc(lo2_mm, 1)

            def retention_turn():
                pe.wait_ge(rot_ok, 1)
                pe.wait_ge(ab_ok, 1)
                pe.wait_ge(lo_ok, 1)
                for u, src in enumerate((QR, KR)):
                    for a in range(TT):
                        for h in range(RH):
                            last = nc.tensor.transpose(bank[3 + 2 * u + a][:, h * P:(h + 1) * P], src[:, a, h * P:(h + 1) * P], ident)
                last.then_inc(rt_mm, 1)

            def retention_scores():
                pe.wait_ge(sig_ok, 2)
                for a, bk in ((0, 7), (1, 3)):
                    for h in range(RH):
                        mm(bank[bk][:, h * P:(h + 1) * P], KT[:, a, h, :], QT[:, a, h, :], start=True, stop=True, skip_group_check=True)
                for h in range(RH):
                    last = mm(bank[4][:, h * P:(h + 1) * P], KD0[:, h * P:(h + 1) * P], TM[:, 0, 2 * RT + h * P:2 * RT + (h + 1) * P],
                              start=True, stop=True, skip_group_check=True)
                last.then_inc(rt_mm, 1)

            def retention_values():
                pe.wait_ge(rt_dve, 1)
                for a in range(TT):
                    for h in range(RH):
                        mm(bank[5 + a][:, h * P:(h + 1) * P], ST[:, a, h, :], TM[:, a, 2 * RT + h * P:2 * RT + (h + 1) * P],
                           start=True, stop=True, skip_group_check=True)
                for h in range(RH):
                    last = mm(bank[7][:, h * P:(h + 1) * P], QT[:, 1, h, :], KV0[:, h * P:(h + 1) * P],
                              start=True, stop=True, skip_group_check=True)
                last.then_inc(rt_mm, 1)

            def gate_sums():
                pe.wait_ge(gate_ok, 1)
                for a in range(TT):
                    mm(bank[6][:, a * 6:a * 6 + 6], con("incl"), gate[:, a * 6:a * 6 + 6], start=True, stop=True, skip_group_check=True)
                    mm(bank[6][:, 12 + a * 6:12 + a * 6 + 6], con("after"), gate[:, a * 6:a * 6 + 6], start=True, stop=True, skip_group_check=True)
                for m in range(12):
                    last = mm(bank[3 + m // 4][:, (m % 4) * P:(m % 4 + 1) * P], GTMP1[:, m, :], con("incl"), start=True, stop=True, skip_group_check=True)
                last.then_inc(gate_mm, 1)

            def beta_rows():
                pe.wait_ge(gexp_ok, 1)
                for m in range(12):
                    last = mm(bank[3 + m // 4][:, (m % 4) * P:(m % 4 + 1) * P], GTMP2[:, m, :], ident, start=True, stop=True, skip_group_check=True)
                last.then_inc(gate_mm, 1)

            def gdn_lengths(i):
                pe.wait_ge(conv_ok, i + 1)
                if i:
                    pe.wait_ge(gn_ok, i)
                else:
                    pe.wait_ge(gexp_ok, 2)
                channel_sums(con("ones"), CSQ, (3, 4, 5)).then_inc(sq_mm, 1)

            def kk_lengths():
                pe.wait_ge(sq_ok, 1)
                pe.wait_ge(prod_ok, 6)
                channel_sums(con("bd"), T2, (3, 4, 5)).then_inc(sq_mm, 1)

            def gdn_products():
                pe.wait_ge(gn_ok, 2)
                p = 0
                for g in range(3):
                    for rhs in (gq, gk):
                        if p >= 5:
                            pe.wait_ge(prod_ok, p - 4)

                        def pair(q, g=g, rhs=rhs):
                            h, a = 2 * g + q // 2, q % 2
                            return gk[:, h, a * P:(a + 1) * P], rhs[:, h, a * P:(a + 1) * P]
                        product(p, 3 + p % 5, pair)
                        p += 1

            after = {NTOK - 1: (low_rank_and_ab,), NTOK: (retention_turn,), NTOK + 1: (lambda: low_rank_out(0),),
                     NTOK + 2: (lambda: low_rank_out(1),), NTOK + 3: (retention_scores,),
                     NTOK + 4: (retention_values,), NTOK + 6: (gate_sums,), NTOK + 8: (beta_rows,),
                     NTOK + 10: (lambda: gdn_lengths(0),), NTOK + 13: (lambda: gdn_lengths(1),),
                     NTOK + 16: (gdn_products,), NTOK + 20: (kk_lengths,)}
            for n in range(NCHUNK):
                if n >= 3:
                    pe.wait_ge(win_out, n - 2)
                pe.wait_ge(win_in[n % 3], 16 * (n // 3 + 1))
                (win_token if n < NTOK else win_chan)(n % 3)
                for step in after.get(n, ()):
                    step()
            pe.wait_ge(bon_ok, 1)
            channel_sums(con("bd"), T4, (5, 6, 7)).then_inc(bon_mm, 1)

            def to_tokens(u, src):
                for a in range(TT):
                    if u + a == 2:
                        pe.wait_ge(bon_done, 1)
                    if u + a >= 4:
                        pe.wait_ge(tok_a, min(u + a - 3, 8))
                    for j in range(6):
                        bk = bank[2 * ((u + a) % 4) + j // 4]
                        last = nc.tensor.transpose(bk[:, (j % 4) * P:(j % 4 + 1) * P], src[:, j, a * P:(a + 1) * P], ident)
                    last.then_inc(tok_mm, 1)

            pe.wait_ge(chan_ok, 1)
            pe.wait_ge(win_out, 32)
            for u, src in ((0, T3), (2, T5), (4, pv), (6, T1)):
                to_tokens(u, src)

            pe.wait_ge(tok_a, 8)
            p = 6
            for u, src in ((8, gk), (10, gv)):
                to_tokens(u, src)

            for bt in range(3):
                if bt == 2:
                    pe.wait_ge(u2_ok, bt)
                if bt < 2:
                    hh = bt
                    rows = slice(hh * CH, (hh + 1) * CH)
                    for g in range(3):
                        for lhs, rhs in ((T2, T1), (pk, T1), (T2, pr), (pk, pr)):
                            def pair(q, g=g, lhs=lhs, rhs=rhs):
                                j, a = 2 * g + q // 2, q % 2
                                return lhs[rows, j, a * P:(a + 1) * P], rhs[rows, j, a * P:(a + 1) * P]
                            if p == 21:
                                pe.wait_ge(u2_ok, 1)
                            if p >= 14:
                                pe.wait_ge(prod_ok, p - 7)
                            elif p % 2 == 0:
                                pe.wait_ge(tok_d, p // 2 - 2)
                            product(p, product_bank(p), pair)
                            p += 1
                    pe.wait_ge(prod_ok, p)
                for g in range(3):
                    pe.wait_ge(t0_ok, 3 * bt + g + 1)
                    for q in range(4):
                        last = nc.tensor.transpose(bank[2 * g + 1][:, q * P:(q + 1) * P], TI3[:, g, q * P:(q + 1) * P], ident)
                    last.then_inc(t0_mm, 1)
                for lv in range(1, LEVELS):
                    n = (bt * (LEVELS - 1) + lv - 1) * 3
                    for g in range(3):
                        pe.wait_ge(lm_ok, n + g + 1)
                        if lv == 1:
                            pe.wait_ge(t0_sb, 3 * bt + g + 1)
                        elif lv > 1:
                            pe.wait_ge(t_ok, n - 3 + g + 1)
                        for q in range(4):
                            c = slice(q * P, (q + 1) * P)
                            last = mm(bank[2 * g][:, c], LM3[:, g, c], TM3[:, g, c], start=True, stop=True, skip_group_check=True)
                        last.then_inc(a_mm, 1)
                    for g in range(3):
                        pe.wait_ge(a_sb, n + g + 1)
                        for q in range(4):
                            c = slice(q * P, (q + 1) * P)
                            if lv < LEVELS - 1:
                                mm(bank[2 * g + 1][:, c], TI3[:, g, c], AS3[:, g, c], start=True, stop=True, skip_group_check=True)
                            last = mm(bank[2 * g][:, c], AS3[:, g, c], TI3[:, g, c], start=True, stop=True, skip_group_check=True)
                        last.then_inc(t_mm, 1)
                pe.wait_ge(t_ok, 3 * (LEVELS - 1) * (bt + 1))
                if bt < 2:
                    for g in range(3):
                        for q in range(4):
                            j, a = 2 * g + q // 2, q % 2
                            c0 = (g % 2) * 256 + q * CH
                            last = mm(bank[g // 2][:, c0:c0 + CH], LK3[:, g, q * P:(q + 1) * P],
                                      tok(T3)[:, a, j * P + hh * CH:j * P + (hh + 1) * CH],
                                      start=True, stop=True, skip_group_check=True)
                    last.then_inc(u1_mm, 1)
                    pe.wait_ge(u1_ok, bt + 1)
                    for g in range(3):
                        for q in range(4):
                            j, a = 2 * g + q // 2, q % 2
                            c0 = (g % 2) * 256 + q * CH
                            mm(bank[2 + g // 2][:, c0:c0 + CH], TI3[:, g, q * P:(q + 1) * P], X1[:, g, q * CH:(q + 1) * CH],
                               start=True, stop=True, skip_group_check=True)
                            last = mm(bank[4 + g][rows, q * P:(q + 1) * P],
                                      tok(T5)[:, a, j * P + hh * CH:j * P + (hh + 1) * CH], TI3[:, g, q * P:(q + 1) * P],
                                      start=True, stop=True, skip_group_check=True)
                    last.then_inc(u2_mm, 1)
                else:
                    for g in range(3):
                        for q in range(4):
                            h, a = 2 * g + q // 2, q % 2
                            m = h * 2 + a
                            mm(bank[2 * a + h // 4][:, (h % 4) * P:(h % 4 + 1) * P], TI3[:, g, q * P:(q + 1) * P],
                               VBG[:, a, h * P:(h + 1) * P], start=True, stop=True, skip_group_check=True)
                            last = mm(bank[4 + m // 4][:, (m % 4) * P:(m % 4 + 1) * P], tok(gk)[:, a, h * P:(h + 1) * P],
                                      TI3[:, g, q * P:(q + 1) * P], start=True, stop=True, skip_group_check=True)
                    last.then_inc(u2_mm, 1)
            pe.wait_ge(u2_ok, 3)

            kinds = ((0, T1, M1, pr), (2, WTG, S1, gq))
            for c in range(NC):
                a, base = c // 2, CH * (c % 2)
                rows, cols_ = slice(base, base + CH), slice(a * P + base, a * P + base + CH)
                pe.wait_ge(m_ok, c + 1)
                for b0, wt, st, _ in kinds:
                    for j in range(6):
                        last = mm(bank[b0 + j // 4][rows, (j % 4) * P:(j % 4 + 1) * P], wt[:, j, cols_], st[:, j, :],
                                  start=True, stop=True, skip_group_check=True)
                last.then_inc(su_mm, 1)
                if c == 2:
                    pe.wait_ge(so_ok, 1)
                for b0, _, st, rd in kinds:
                    for j in range(6):
                        last = mm(bank[4 + b0 + j // 4][rows, (j % 4) * P:(j % 4 + 1) * P], rd[:, j, cols_], st[:, j, :],
                                  start=(j % 4 == 0), stop=False, skip_group_check=True)
                last.then_inc(sx_mm, 1)
                pe.wait_ge(su_ok, c + 1)
                if c < NC - 1:
                    for j in range(6):
                        o = bank[j // 4][:, (j % 4) * P:(j % 4 + 1) * P]
                        cj = slice(j * P, (j + 1) * P)
                        mm(o, tok(T6)[rows, a, cj], tok(T2)[rows, a, cj], start=(j % 4 == 0), stop=False, skip_group_check=True)
                        mm(o, tok(T7)[rows, a, cj], tok(T3)[rows, a, cj], start=False, stop=True, skip_group_check=True)
                    for j in range(6):
                        cj = slice(j * P, (j + 1) * P)
                        last = mm(bank[2 + j // 4][:, (j % 4) * P:(j % 4 + 1) * P], KDG[rows, a, cj], VBG[rows, a, cj],
                                  start=True, stop=True, skip_group_check=True)
                    last.then_inc(sm_mm, 1)
                if c % 2:
                    for j in range(6):
                        for hh in range(2):
                            g, q = hh * 3 + j // 2, (j % 2) * 2 + a
                            cj = slice(j * P + hh * CH, j * P + (hh + 1) * CH)
                            o = bank[4 + j // 4][:, (j % 4) * P + hh * CH:(j % 4) * P + (hh + 1) * CH]
                            mm(o, RB[:, g, q * P:(q + 1) * P], tok(T2)[:, a, cj], start=False, stop=False, skip_group_check=True)
                            mm(o, RK[:, g, q * P:(q + 1) * P], tok(T3)[:, a, cj], start=False, stop=True, skip_group_check=True)
                    for h in range(6):
                        last = mm(bank[6 + h // 4][:, (h % 4) * P:(h % 4 + 1) * P], DT[:, h * 2 + a, :],
                                  VBG[:, a, h * P:(h + 1) * P], start=False, stop=True, skip_group_check=True)
                    last.then_inc(so_mm, 1)

            def head_transposes(banks, j0, src):
                for i, bk in enumerate(banks):
                    for j in range(j0 + 2 * i, j0 + 2 * i + 2):
                        for a in range(TT):
                            o = (j % 2) * T + a * P
                            last = nc.tensor.transpose(bank[bk][:, o:o + P], src(a, j), ident)
                return last

            def project(i, tiles):
                k = ORDER[i]
                pe.wait_ge(wo_in[i % 6], 16 * (i // 6 + 1))
                for a in tiles:
                    for n in range(4):
                        last = mm(bank[a * 4 + n][:], MIX[:, k, a * P:(a + 1) * P], WO[i % 6][:, n * 512:(n + 1) * 512],
                                  start=(i == 0), stop=(i == K - 1))
                    if i == K - 1:
                        last.then_inc(wo_tile, 1)
                if tiles[-1] == 1:
                    if i < K - 1:
                        last.then_inc(wo_mm, 1)

            head_transposes((0, 1), 0, lambda a, j: YR[:, a * RH + j, :]).then_inc(mt_mm, 1)
            pe.wait_ge(mt_ok, 1)
            for i in range(RH):
                project(i, (0,))
            pe.wait_ge(o_ok, 1)
            pe.wait_ge(so_ok, 2)
            head_transposes((4, 5, 6), 0, lambda a, j: tok(pk)[:, a, j * P:(j + 1) * P]).then_inc(mt_mm, 1)
            pe.wait_ge(o_ok, 2)
            og = lambda a, j: OG[:, a, j * P:(j + 1) * P]
            head_transposes((7,), 0, og)
            pe.wait_ge(mt_ok, 2)
            head_transposes((4, 5), 2, og).then_inc(mt_mm, 1)
            for i in (4, 5):
                project(i, (0,))
            pe.wait_ge(mt_ok, 3)
            for i in range(6):
                project(i, (1,))
            for i in range(6, K):
                project(i, (0, 1))

            pe.wait_ge(xs_ok, 1)
            pe.wait_ge(rw_in, 16)
            xs = XS.rearrange("p a (d k) -> p a k d", k=K)

            def logits(r):
                pe.wait_ge(xs_t, r + 1)
                for k in (2 * r, 2 * r + 1):
                    for a in range(TT):
                        last = mm(bank[4 + a][:, 0:36], XTT[:, k, a * P:(a + 1) * P], RWT[:, k, :], start=(k == 0), stop=(k == K - 1))
                return last

            for r in range(8):
                if r >= 2:
                    logits(r - 2)
                for kk in range(2):
                    for a in range(TT):
                        o = kk * T + a * P
                        last = nc.tensor.transpose(bank[r % 4][:, o:o + P], xs[:, a, 2 * r + kk, :], ident)
                last.then_inc(xs_mm, 1)
            logits(6)
            logits(7).then_inc(lg_mm, 1)
            pe.wait_ge(e_ok, 1)
            mm(bank[6][:, 0:32], con("before"), R1[:, 0, :], start=True, stop=True, skip_group_check=True)
            mm(bank[6][:, 32:64], con("ones"), R1[:, 0, :], start=True, stop=False, skip_group_check=True)
            mm(bank[6][:, 32:64], con("before"), R1[:, 1, :], start=False, stop=True, skip_group_check=True)
            mm(bank[6][:, 64:96], con("ones"), R1[:, 0, :], start=True, stop=False, skip_group_check=True)
            mm(bank[6][:, 64:96], con("ones"), R1[:, 1, :], start=False, stop=True, skip_group_check=True).then_inc(pos_mm, 1)

            def quad_of_experts(r, i, ahead):
                def up(b):
                    s = b % 2
                    pe.wait_ge(wu_in[s], (r * 16 + i * 2) * 32 + 32 * (b // 2 + 1))
                    if b >= 2:
                        pe.wait_ge(up_sb, r * NE + i * 4 + (b - 1))
                    for k in range(K):
                        j = k % 4
                        for w in range(2):
                            last = mm(bank[s][32 * j:32 * j + 32, w * HID:(w + 1) * HID], XQ[:, k, b * TOPC:(b + 1) * TOPC], WU[s][:, w, k, :],
                                      start=(k < 4 and w == 0), stop=(k >= 12), skip_group_check=True)
                    last.then_inc(up_mm, 1)
                    pe.wait_ge(up_mm, r * NE + i * 4 + (b + 1))
                    pe.sem_inc(wu_free[s], 1)

                def hidden(b):
                    pe.wait_ge(up_sb, r * NE + i * 4 + (b + 1))
                    if b >= 1:
                        pe.wait_ge(hd_ok, r * NE + i * 4 + b)
                    for c in range(4):
                        last = mm(bank[2][:, c * TOPC:(c + 1) * TOPC], UP[b % 2][:, c * P:(c + 1) * P], stack,
                                  start=True, stop=True, skip_group_check=True)
                    last.then_inc(h_mm, 1)

                def down(b):
                    s = b % 2
                    pe.wait_ge(hd_ok, r * NE + i * 4 + (b + 1))
                    pe.wait_ge(wd_in[s], (r * 16 + i * 2) * 16 + 16 * (b // 2 + 1))
                    for n in range(4):
                        for f in range(2):
                            last = mm(bank[3 + n][32 * b:32 * b + 32, :], HD[s][:, f, :], WD[s][:, f, n * 512:(n + 1) * 512],
                                      start=(f == 0), stop=(f == 1), skip_group_check=True)
                    last.then_inc(dn_mm, 1)
                    pe.wait_ge(dn_mm, r * NE + i * 4 + (b + 1))
                    pe.sem_inc(wd_free[s], 1)

                pe.wait_ge(xq_ok, r * 8 + i + 1)
                up(0)
                up(1)
                hidden(0)
                if ahead:
                    gather(r, i + 1, 0)
                down(0)
                up(2)
                hidden(1)
                if ahead:
                    gather(r, i + 1, 1)
                down(1)
                up(3)
                hidden(2)
                if ahead:
                    gather(r, i + 1, 2)
                down(2)
                hidden(3)
                if ahead:
                    gather(r, i + 1, 3)
                down(3)
                pe.wait_ge(sgq_ok, r * 8 + i + 1)
                pe.wait_ge(ya_ok, r * 8 + i + 1)
                pe.wait_ge(yd_ok, r * 8 + i + 1)
                if ahead:
                    pe.wait_ge(g_ok, r * 32 + i * 4 + 8)
                for q in range(8):
                    a, n = q // 4, q % 4
                    if q >= 2:
                        pe.wait_ge(sc_ok, (r * 8 + i) * 8 + (q - 1))
                    mm(bank[7 if q % 2 else 2][:], SGQ[:, a * P:(a + 1) * P], YS[:, n * 512:(n + 1) * 512],
                       start=True, stop=True).then_inc(sc_mm, 1)
                pe.wait_ge(sc_ok, (r * 8 + i) * 8 + 8)

            def gather(r, quad, c, bk=7):
                if bk == 7:
                    pe.wait_ge(g_ok, r * 32 + quad * 4 + c)
                col0 = quad * 4 * TOPC
                cs = slice(col0, col0 + 4 * TOPC) if isinstance(quad, int) else bass.ds(col0, 4 * TOPC)
                for kk in range(4):
                    for a in range(TT):
                        last = mm(bank[bk][:, kk * P:(kk + 1) * P], xs[:, a, 4 * c + kk, :], PS[:, a, cs],
                                  start=(a == 0), stop=(a == TT - 1), skip_group_check=True)
                last.then_inc(g_mm, 1)

            def experts(r):
                pe.wait_ge(p_ok, r + 1)
                for c in range(4):
                    gather(r, 0, c, 3 + c)
                pe.wait_ge(pg_ok, r + 1)
                for i in range(4):
                    bk = (0, 1, 2, 7)[i]
                    for qd in range(2):
                        for a in range(TT):
                            o = qd * T + a * P
                            last = nc.tensor.transpose(bank[bk][:, o:o + P], PG[:, a, (2 * i + qd) * P:(2 * i + qd + 1) * P], ident)
                    last.then_inc(sg_mm, 1)
                with pe.Fori(0, 7) as i:
                    quad_of_experts(r, i, True)
                quad_of_experts(r, 7, False)

            experts(0)
            pe.wait_ge(flag_ok, 1)
            with pe.If(pe.value_load(flag[0:1, 0:1]) == 1):
                with pe.Fori(1, PASSES) as r:
                    experts(r)

        @block.scalar
        def _(eng):
            f = nc.scalar.activation
            done = Steps(eng, act)
            cp = ACT.Copy

            def root(n, ap):
                eng.wait_ge(ss_ok, n)
                f(ap, ap, ACT.Sqrt).then_inc(std_ok, 1)

            root(1, rstd)
            eng.wait_ge(ang_ok, 1)
            done(f(SIN, ANG, ACT.Sin))
            f(COS, ANR, ACT.Sin).then_inc(sin_ok, 1)

            eng.wait_ge(xt_mm, 8)

            def evac(n):
                eng.wait_ge(win_mm, n + 1)
                if n < NTOK:
                    f(TM[:, :, n * CW:(n + 1) * CW], bank[n % 3][:].rearrange("p (a c) -> p a c", a=TT), cp).then_inc(win_out, 1)
                else:
                    t = SEGMENTS[(n - NTOK) // 3][0] + 2 * ((n - NTOK) % 3)
                    f(PJ[:, t:t + 2, :].rearrange("p a b -> p (a b)"), bank[n % 3][:], cp).then_inc(win_out, 1)

            def low_rank():
                eng.wait_ge(ab_mm, 1)
                f(AB, bank[3][:, 0:24].rearrange("p (a c) -> p a c", a=TT), cp).then_inc(ab_ok, 1)
                eng.wait_ge(lo_mm, 1)
                done(f(LH[0:96, 0, :], bank[4][0:96, 0:T], ACT.Tanh))
                f(LH[0:96, 1, :], bank[4][0:96, T:2 * T], cp).then_inc(lo_ok, 1)

            def retention_turned():
                eng.wait_ge(rt_mm, 1)
                for u, dst in enumerate((QT, KT)):
                    for a in range(TT):
                        done(f(dst[:, a].rearrange("p h c -> p (h c)"), bank[3 + 2 * u + a][:], cp))
                eng.sem_inc(rt_ok, 1)

            def low_rank_gates(fct):
                for half in range(3):
                    eng.wait_ge(lo2_mm, fct * 3 + half + 1)
                    for jj in range(2):
                        j = half * 2 + jj
                        done(f((T3, T4)[fct][:, j, :], bank[5 + half][:, jj * T:(jj + 1) * T], ACT.Sigmoid,
                               bias=pcol(("w0", "a0")[fct], j)))
                eng.sem_inc(sig_ok, 1)

            def retention_inner():
                eng.wait_ge(rt_mm, 3)
                for a in range(TT):
                    done(f(YR[:, a * RH:(a + 1) * RH, :].rearrange("p h c -> p (h c)"), bank[5 + a][:], cp))
                eng.sem_inc(rt_ok, 1)

            def gate_functions():
                eng.wait_ge(ga_ok, 1)
                done(f(stat[:, 0:12], stat[:, 0:12], ACT.Exp, scale=-1.0))
                done(f(ea, pcol("alog", 0, 6), ACT.Exp))
                done(f(stat[:, 0:12], stat[:, 0:12], ACT.Ln, bias=1.0))
                done(f(beta.rearrange("p (a b) -> p a b", a=TT), AB[:, :, 6:12], ACT.Sigmoid))
                eng.sem_inc(gb_ok, 1)

            def gate_exps():
                eng.wait_ge(gexp_in, 1)
                done(f(DT, DT, ACT.Exp))
                done(f(egc, gcum, ACT.Exp))
                done(f(ekd, bank[6][:, 12:24], ACT.Exp))
                eg = EG.rearrange("p a b -> p (a b)")
                for i in range(3):
                    done(f(eg[:, i * 512:(i + 1) * 512], bank[3 + i][:], ACT.Exp))
                eng.sem_inc(gexp_ok, 1)

            def conv_silu(s):
                eng.wait_ge(conv_in, s + 1)
                f((gq, gk, gv)[s], CACC, ACT.Silu).then_inc(silu_ok, 1)

            def lengths(n, dst, ok):
                eng.wait_ge(sq_mm, n)
                flat = dst.rearrange("p a b -> p (a b)")
                for i in range(3):
                    done(f(flat[:, i * 512:(i + 1) * 512], bank[3 + i][:], ACT.Sqrt, bias=eps6))
                eng.sem_inc(ok, 1)

            def rwkv_decays():
                eng.wait_ge(cum_ok, 1)
                done(f(T6, T6, ACT.Exp, scale=-DECAY))
                done(f(T7, T5, ACT.Exp, scale=-DECAY))
                done(f(T3, T5, ACT.Exp, scale=DECAY))
                eng.sem_inc(exp_ok, 1)

            after = {NTOK - 1: (low_rank,), NTOK: (retention_turned,), NTOK + 1: (lambda: low_rank_gates(0),),
                     NTOK + 2: (lambda: low_rank_gates(1),), NTOK + 4: (retention_inner,),
                     NTOK + 5: (lambda: root(2, stat2[:, 0:8]), gate_functions), NTOK + 6: (lambda: conv_silu(0), ),
                     NTOK + 7: (gate_exps,),
                     NTOK + 11: (lambda: lengths(1, CSQ, gs_root), lambda: conv_silu(1)),
                     NTOK + 14: (lambda: lengths(2, CSQ, gs_root), lambda: conv_silu(2)),
                     NTOK + 16: (rwkv_decays,), NTOK + 21: (lambda: lengths(3, T2, exp_ok),)}
            for n in range(NCHUNK):
                evac(n)
                for step in after.get(n, ()):
                    step()
            eng.wait_ge(win_out, NCHUNK)
            for u, dst in enumerate((T6, T6, T7, T7, T3, T3, T5, T5)):
                eng.wait_ge(tok_mm, u + 1)
                b0 = 2 * (u % 4)
                if u == 6:
                    eng.wait_ge(bon_done, 1)
                done(f(tok(dst)[:, u % 2, 0:512], bank[b0][:], cp))
                done(f(tok(dst)[:, u % 2, 512:768], bank[b0 + 1][:, 0:256], cp))
                eng.sem_inc(tok_a, 1)
            eng.wait_ge(pg_mixed, 1)
            done(f(pg, pg, ACT.Sigmoid))
            done(f(gz, gz, ACT.Silu))
            done(f(rg, rg, ACT.Silu))
            eng.sem_inc(gates_ok, 1)
            for bt in range(3):
                for g in range(3):
                    eng.wait_ge(t0_mm, bt * 3 + g + 1)
                    f(TM3[:, g, :], bank[2 * g + 1][:], cp).then_inc(t0_sb, 1)
                for lv in range(1, LEVELS):
                    n = (bt * (LEVELS - 1) + lv - 1) * 3
                    for g in range(3):
                        eng.wait_ge(a_mm, n + g + 1)
                        f(AS3[:, g, :], bank[2 * g][:], cp).then_inc(a_sb, 1)
                if bt < 2:
                    rows = slice(bt * CH, (bt + 1) * CH)
                    eng.wait_ge(u1_mm, bt + 1)
                    x1 = X1.rearrange("p a b -> p (a b)")
                    done(f(x1[:, 0:512], bank[0][:], cp, scale=-1.0))
                    done(f(x1[:, 512:768], bank[1][:, 0:256], cp, scale=-1.0))
                    eng.sem_inc(u1_ok, 1)
                    eng.wait_ge(u2_mm, bt + 1)
                    u0 = tok(pv).rearrange("p a (j h c) -> p a j h c", j=NJ, h=2)
                    for g in range(3):
                        ps = bank[2 + g // 2][:, (g % 2) * 256:(g % 2) * 256 + 256].rearrange("p (j a c) -> p j a c", j=2, a=TT)
                        for a in range(TT):
                            done(f(u0[:, a, 2 * g:2 * g + 2, bt, :], ps[:, :, a, :], cp))
                        done(f(T1[rows, 2 * g:2 * g + 2, :].rearrange("p a b -> p (a b)"), bank[4 + g][rows, :], cp))
                    eng.sem_inc(u2_ok, 1)
                else:
                    eng.wait_ge(u2_mm, 3)
                    for a in range(TT):
                        done(f(tok(gv)[:, a, 0:512], bank[2 * a][:], cp))
                        done(f(tok(gv)[:, a, 512:768], bank[2 * a + 1][:, 0:256], cp))
                    wt = WTG.rearrange("p a b -> p (a b)")
                    for i in range(3):
                        done(f(wt[:, i * 512:(i + 1) * 512], bank[4 + i][:], cp))
                    eng.sem_inc(u2_ok, 1)
            for a in range(TT):
                eng.wait_ge(so_mm, a + 1)
                for b0, dst in ((4, tok(pk)), (6, OG)):
                    done(f(dst[:, a, 0:512], bank[b0][:], cp))
                    done(f(dst[:, a, 512:768], bank[b0 + 1][:, 0:256], cp))
                eng.sem_inc(so_ok, 1)
            root(3, stat2)
            root(4, stat[:, 0:12])
            root(5, rstd)
            eng.wait_ge(rex_in, 1)
            f(R2[:, :, 0:4], R1[:, :, 0:4], ACT.Exp).then_inc(rex_ok, 1)
            eng.wait_ge(rex_in, 2)
            f(stat2[:, 0:2], stat2[:, 0:2], ACT.Exp).then_inc(rex_ok, 1)

            def quad_of_experts(r, i, ahead):
                def up_copy(b):
                    eng.wait_ge(up_mm, r * NE + i * 4 + (b + 1))
                    if b >= 2:
                        eng.wait_ge(h_mm, r * NE + i * 4 + (b - 1))
                    f(UP[b % 2], bank[b % 2][:], cp).then_inc(up_sb, 1)

                def silu(b):
                    eng.wait_ge(h_mm, r * NE + i * 4 + (b + 1))
                    if b >= 1:
                        eng.wait_ge(hd_ok, r * NE + i * 4 + b)
                    f(GS, bank[2][:, 0:64], ACT.Silu).then_inc(gs_ok, 1)

                up_copy(0)
                up_copy(1)
                silu(0)
                up_copy(2)
                silu(1)
                up_copy(3)
                silu(2)
                silu(3)
                eng.wait_ge(dn_mm, r * NE + i * 4 + 4)
                f(YS[:, 0:512], bank[3][:], cp).then_inc(ya_half, 1)
                eng.wait_ge(ya_half, r * 8 + i + 1)
                f(YS[:, 512:1024], bank[4][:], cp).then_inc(ya_ok, 1)

            def experts(r):
                for i in range(4):
                    eng.wait_ge(sg_mm, r * 4 + (i + 1))
                    f(SG[:, 2 * i:2 * i + 2, :].rearrange("p a b -> p (a b)"), bank[(0, 1, 2, 7)[i]][:], cp).then_inc(sg_ok, 1)
                with eng.Fori(0, 7) as i:
                    quad_of_experts(r, i, True)
                quad_of_experts(r, 7, False)

            experts(0)
            eng.wait_ge(flag_ok, 1)
            with eng.If(eng.value_load(flag[0:1, 0:1]) == 1):
                with eng.Fori(1, PASSES) as r:
                    experts(r)
            root(6, rstd)

        @block.vector
        def _(eng):
            v = nc.vector
            done = Steps(eng, dve)
            tt, ts, stt = v.tensor_tensor, v.tensor_scalar, v.scalar_tensor_tensor
            MUL, ADD, SUB, MAX, MIN, EQ = ALU.mult, ALU.add, ALU.subtract, ALU.max, ALU.min, ALU.is_equal

            def rms(n, src, junk):
                for a in range(TT):
                    if n == 1:
                        eng.wait_ge(x_in[a], 16)
                    done(v.tensor_tensor_reduce(junk(a), src[:, a], src[:, a], 1.0, 0.0, MUL, ADD, ssq[:, a:a + 1]))
                done(ts(rstd, ssq, 1.0 / D, 1e-6, MUL, ADD))
                eng.sem_inc(ss_ok, 1)
                eng.wait_ge(std_ok, n)
                done(v.reciprocal(rstd, rstd))

            done(v.memset(eps6, 1e-6))
            rms(1, X, lambda a: XN[:, a])
            for a in range(TT):
                done(ts(XN[:, a], X[:, a], rstd[:, a:a + 1], None, MUL))
            eng.sem_inc(xn_ok, 1)
            eng.wait_ge(c_in, 32)
            for r in range(8):
                eng.wait_ge(xt_mm, r + 1)
                for kk in range(2):
                    k = 2 * r + kk
                    done(ts(HT[:, k, :], bank[3 + r % 4][:, kk * T:(kk + 1) * T], pcol("norm1", k), None, MUL))
                eng.sem_inc(ht_ok, 1)

            eng.wait_ge(tables_in, 32)
            done(v.tensor_copy(posf, posi[:]))
            c1 = 6.28125
            c2 = round((2 * np.pi - c1) * 2 ** 19) / 2 ** 19
            c3 = 2 * np.pi - c1 - c2
            magic = 1.5 * 2 ** 23
            turns = RTMP[:, 0:P].rearrange("p (a b) -> p a b", a=TT)
            for a in range(TT):
                done(ts(ANG[:, a], con("freq"), posf[:, a:a + 1], None, MUL))
            done(v.tensor_copy(ANR, ANG))
            for dst, quarter in ((ANR, 0.25), (ANG, 0.0)):
                done(ts(turns, dst, 1.0 / (2 * np.pi), quarter, MUL, ADD))
                done(ts(turns, turns, magic, None, ADD))
                done(ts(turns, turns, magic, None, SUB))
                for c in (c1, c2, c3):
                    done(stt(dst, turns, -c, dst, MUL, ADD))
                done(ts(dst, dst, quarter * 2 * np.pi, None, ADD))
                done(ts(dst, dst, PI_LO, -PI_LO, MIN, MAX))
            eng.sem_inc(ang_ok, 1)

            done(tt(DH[:, :, 1:T], HT[:, :, 0:T - 1], HT[:, :, 1:T], SUB))
            done(ts(DH[:, :, 0:1], HT[:, :, 0:1], -1.0, None, MUL))
            for name, dst in (("mu_w", XW), ("mu_a", XA)):
                for k in range(K):
                    done(stt(dst[:, k, :], DH[:, k, :], pcol(name, k), HT[:, k, :], MUL, ADD))
            eng.sem_inc(xwa_ok, 1)

            eng.wait_ge(win_out, NTOK)
            eng.wait_ge(sin_ok, 1)
            tmp = RTMP[:, 0:256].rearrange("p (h c) -> p h c", h=RH)
            for src, dst in ((0, QR), (RT, KR)):
                for a in range(TT):
                    s = TM[:, a, src:src + RT].rearrange("p (h e c) -> p h e c", h=RH, e=2)
                    o = dst[:, a].rearrange("p (h e c) -> p h e c", h=RH, e=2)
                    cos, sin = over(COS[:, a], RH), over(SIN[:, a], RH)
                    for e, op in ((0, SUB), (1, ADD)):
                        done(tt(o[:, :, e, :], s[:, :, e, :], cos, MUL))
                        done(tt(tmp, s[:, :, 1 - e, :], sin, MUL))
                        done(tt(o[:, :, e, :], o[:, :, e, :], tmp, op))
            for h in range(RH):
                done(ts(KD0[:, h * P:(h + 1) * P], KR[:, 0, h * P:(h + 1) * P], con("kdec")[:, h:h + 1], None, MUL))
            eng.sem_inc(rot_ok, 1)
            eng.wait_ge(rt_mm, 2)
            for a, bk in ((0, 7), (1, 3)):
                done(tt(ST[:, a].rearrange("p h c -> p (h c)"), bank[bk][:], con("dmask"), MUL))
            done(v.tensor_copy(KV0, bank[4][:]))
            eng.sem_inc(rt_dve, 1)
            eng.wait_ge(rt_ok, 2)
            for h in range(RH):
                done(stt(YR[:, RH + h, :], bank[7][:, h * P:(h + 1) * P], con("qdec")[:, h:h + 1], YR[:, RH + h, :], MUL, ADD))

            def head_norm(n, y, sq, g, w, st, mean, eps):
                if mean:
                    done(v.tensor_reduce(st, y, AX, ADD))
                    done(ts(st, st, 1.0 / w, None, MUL))
                    done(tt(y, y, wide(st, w), SUB))
                done(tt(sq, y, y, MUL))
                done(v.tensor_reduce(st, sq, AX, ADD))
                done(ts(st, st, 1.0 / w, eps, MUL, ADD))
                eng.sem_inc(ss_ok, 1)
                eng.wait_ge(std_ok, n)
                done(v.reciprocal(st, st))
                done(tt(y, y, wide(st, w), MUL))

            head_norm(2, YR, view(198, 8, P), 8, P, stat2[:, 0:8], True, 1e-5)

            g3 = gate.rearrange("p (a b) -> p a b", a=TT)
            eng.wait_ge(ab_ok, 1)
            done(tt(g3, AB[:, :, 0:6], over(pcol("dt", 0, 6), TT), ADD))
            done(ts(stat[:, 0:12], gate, -1.0, None, MUL))
            done(tt(stat[:, 0:12], stat[:, 0:12], gate, MAX))
            eng.sem_inc(ga_ok, 1)
            eng.wait_ge(gb_ok, 1)
            done(stt(gate, gate, 0.0, stat[:, 0:12], MAX, ADD))
            done(stt(g3, g3, -1.0, over(ea, TT), MUL, MUL))
            g1v = GTMP1.rearrange("p (h a) c -> p h a c", a=TT)
            g2v = GTMP2.rearrange("p (h a) c -> p h a c", a=TT)
            for a in range(TT):
                done(v.tensor_copy(g1v[:, :, a, :], wide(gate[:, a * 6:a * 6 + 6], P)))
                done(v.tensor_copy(g2v[:, :, a, :], wide(beta[:, a * 6:a * 6 + 6], P)))
            eng.sem_inc(gate_ok, 1)

            def conv(s):
                q = (gq, gk, gv)[s]
                eng.wait_ge(win_out, NTOK + 3 * s + 3)
                if s:
                    eng.wait_ge(silu_ok, s)
                for j in range(NH):
                    c = lambda i: pcol("conv", i * 18 + s * 6 + j)
                    done(ts(CACC[:, j, :], q[:, j, :], c(3), None, MUL))
                    for d in (1, 2, 3):
                        done(stt(CACC[:, j, d:T], q[:, j, 0:T - d], c(3 - d), CACC[:, j, d:T], MUL, ADD))
                eng.sem_inc(conv_in, 1)

            def squares(s):
                q = (gq, gk)[s]
                eng.wait_ge(silu_ok, s + 1)
                done(tt(CSQ, q, q, MUL))
                eng.sem_inc(conv_ok, 1)

            def unit(s):
                q = (gq, gk)[s]
                eng.wait_ge(gs_root, s + 1)
                done(v.reciprocal(CSQ, CSQ))
                done(stt(q, q, P ** -0.5 if s == 0 else 1.0, CSQ, MUL, MUL))
                eng.sem_inc(gn_ok, 1)

            conv(0)
            squares(0)
            eng.wait_ge(gate_mm, 1)
            done(v.tensor_copy(gcum, bank[6][:, 0:12]))
            for m in range(12):
                h, a = m // 2, m % 2
                done(ts(DT[:, m, :], bank[3 + m // 4][:, (m % 4) * P:(m % 4 + 1) * P], gcum[:, a * 6 + h:a * 6 + h + 1], 0.0, SUB, MIN))
            eng.sem_inc(gexp_in, 1)
            lg, dt = (q.rearrange("p a b -> p (a b)") for q in (LG, DT))
            conv(1)
            eng.wait_ge(gexp_ok, 1)
            done(tt(DT, DT, over(con("incl"), 12), MUL))
            eng.wait_ge(gate_mm, 2)
            for i in range(3):
                done(tt(lg[:, i * 512:(i + 1) * 512], bank[3 + i][:], dt[:, i * 512:(i + 1) * 512], MUL))
            done(tt(LG, LG, over(con("strict"), 12), MUL))
            done(v.tensor_copy(glast, EG[:, :, CH - 1:T:CH]))
            eng.sem_inc(gexp_ok, 1)
            unit(0)
            squares(1)
            conv(2)
            unit(1)

            for j in range(NJ):
                done(v.tensor_tensor_scan(T5[:, j, :], con("carry"), T3[:, j, :], 0.0, MUL, ADD))
            done(tt(T6, T5, T3, SUB))
            eng.sem_inc(cum_ok, 1)
            eng.wait_ge(silu_ok, 3)

            def shift_mix(i, diff):
                q = (pr, pk, pv, pg)[i]
                eng.wait_ge(win_out, NTOK + (12, 15, 18, 24)[i])
                done(tt(diff[:, :, 1:T], q[:, :, 0:T - 1], q[:, :, 1:T], SUB))
                done(ts(diff[:, :, 0:1], q[:, :, 0:1], -1.0, None, MUL))
                for j in range(NJ):
                    done(stt(q[:, j, :], diff[:, j, :], pcol("mu", i * NJ + j), q[:, j, :], MUL, ADD))

            for i in range(2):
                shift_mix(i, T1)
            for g in range(3):
                for i, dst in enumerate((dt, lg)):
                    p = 2 * g + i
                    eng.wait_ge(prod_mm, p + 1)
                    done(tt(dst[:, g * 512:(g + 1) * 512], bank[3 + p % 5][:], dst[:, g * 512:(g + 1) * 512], MUL))
                    eng.sem_inc(prod_ok, 1)
            done(tt(gq, gq, EG, MUL))
            shift_mix(2, T1)
            for j in range(NJ):
                done(ts(T1[:, j, :], pk[:, j, :], pcol("k_k", j), None, MUL))
            done(tt(T2, T1, T1, MUL))
            eng.sem_inc(sq_ok, 1)
            eng.wait_ge(exp_ok, 2)
            done(v.reciprocal(T2, T2))
            done(tt(T1, T1, T2, MUL))
            done(tt(T2, T1, T4, MUL))
            done(tt(T2, T2, T3, MUL))
            for j in range(NJ):
                done(ts(T4[:, j, :], T4[:, j, :], -1.0, pcol("k_a", j), ADD, MUL))
            done(stt(pk, T4, 1.0, pk, ADD, MUL))
            for j in range(NJ):
                done(stt(T4[:, j, :], pr[:, j, :], pcol("r_k", j), pk[:, j, :], MUL, MUL))
            eng.sem_inc(bon_ok, 1)
            done(tt(T1, T1, T6, MUL))
            done(tt(pr, pr, T7, MUL))
            done(tt(pk, pk, T3, MUL))
            done(v.tensor_copy(elast, T7[:, :, CH - 1:T:CH]))
            for j in range(NJ):
                for src, dst in ((T2, T3), (pk, T5)):
                    done(tt(dst[:, j, :].rearrange("p (c t) -> p c t", c=NC), src[:, j, :].rearrange("p (c t) -> p c t", c=NC),
                            wide(elast[:, j, :], CH), MUL))
            eng.sem_inc(chan_ok, 1)
            eng.wait_ge(bon_mm, 1)
            t4, pvf = (q.rearrange("p a b -> p (a b)") for q in (T4, pv))
            for i in range(3):
                done(tt(t4[:, i * 512:(i + 1) * 512], bank[5 + i][:], pvf[:, i * 512:(i + 1) * 512], MUL))
            eng.sem_inc(bon_done, 1)
            shift_mix(3, view(0, NJ, T))
            eng.sem_inc(pg_mixed, 1)

            done(tt(egc, egc, beta, MUL))
            kbe = tok(gk)
            for u in range(8, 12):
                a, b0 = u % 2, 2 * (u % 4)
                eng.wait_ge(tok_mm, 12 if u < 10 else u + 1)
                for h0, nh, bk in ((0, 4, b0), (4, 2, b0 + 1)):
                    ps = bank[bk][:, 0:nh * P].rearrange("p (h c) -> p h c", h=nh)
                    o = lambda t: t[:, a, h0 * P:(h0 + nh) * P].rearrange("p (h c) -> p h c", h=nh)
                    w = lambda t: wide(t[:, a * 6 + h0:a * 6 + h0 + nh], P)
                    if u < 10:
                        done(tt(o(kbe), ps, w(egc), MUL))
                        done(tt(o(KDG), ps, w(ekd), MUL))
                    else:
                        done(tt(o(VBG), ps, w(beta), MUL))
                eng.sem_inc(tok_d, 1)

            q4 = lambda t, g: t[:, g, :].rearrange("p (q c) -> p q c", q=4)

            def first_merge(g, lt):
                done(tt(q4(TI3, g), q4(lt, g), over(con("lev0"), 4), MUL))
                done(tt(q4(TI3, g), over(con("ident"), 4), q4(TI3, g), SUB))
                eng.sem_inc(t0_ok, 1)

            p = 6
            for bt in range(3):
                lt = LT3 if bt < 2 else LG.rearrange("p (g q) c -> p g (q c)", g=3)
                if bt < 2:
                    if bt:
                        eng.wait_ge(u1_mm, bt)
                        eng.wait_ge(u2_mm, bt)
                        eng.wait_ge(lm_ok, 3 * (LEVELS - 1) * bt)
                    for g in range(3):
                        gg = bt * 3 + g
                        for dst, mask in ((LT3[:, g, :], "strict"), (LK3[:, g, :], "strict"), (RB[:, gg, :], "incl"), (RK[:, gg, :], "incl")):
                            eng.wait_ge(prod_mm, p + 1)
                            done(tt(dst.rearrange("p (q c) -> p q c", q=4), bank[product_bank(p)][:].rearrange("p (q c) -> p q c", q=4),
                                    over(con(mask), 4), MUL))
                            eng.sem_inc(prod_ok, 1)
                            p += 1
                        first_merge(g, lt)
                else:
                    eng.wait_ge(u2_mm, bt)
                    for g in range(3):
                        first_merge(g, lt)
                for lv in range(1, LEVELS):
                    n = (bt * (LEVELS - 1) + lv - 1) * 3
                    for g in range(3):
                        eng.wait_ge(t_mm, n + g + 1)
                        if lv < LEVELS - 1:
                            done(tt(TM3[:, g, :], TM3[:, g, :], bank[2 * g + 1][:], SUB))
                        done(tt(TI3[:, g, :], TI3[:, g, :], bank[2 * g][:], SUB))
                        eng.sem_inc(t_ok, 1)

            eng.wait_ge(u2_ok, 3)
            done(v.memset(M1, 0.0))
            done(v.memset(S1, 0.0))
            eng.sem_inc(m_ok, 1)
            for c in range(NC):
                a, base = c // 2, CH * (c % 2)
                rows = slice(base, base + CH)
                eng.wait_ge(su_mm, c + 1)
                for b0, u0, u in ((0, tok(pv), tok(T2)), (2, tok(gv), VBG)):
                    done(tt(u[rows, a, 0:512], u0[rows, a, 0:512], bank[b0][rows, :], SUB))
                    done(tt(u[rows, a, 512:768], u0[rows, a, 512:768], bank[b0 + 1][rows, 0:256], SUB))
                eng.sem_inc(su_ok, 1)
                if c == NC - 1:
                    break
                eng.wait_ge(sx_mm, c + 1)
                done(tt(M1, M1, wide(elast[:, :, c], P), MUL))
                done(tt(S1, S1, wide(glast[:, :, c], P), MUL))
                eng.wait_ge(sm_mm, c + 1)
                for j0, nj, bk in ((0, 4, 0), (4, 2, 1)):
                    done(tt(MTMP[:, j0:j0 + nj, :], bank[bk][:, 0:nj * P].rearrange("p (j c) -> p j c", j=nj), over(con("bd"), nj), MUL))
                done(tt(M1, M1, MTMP, ADD))
                for j0, nj, bk in ((0, 4, 2), (4, 2, 3)):
                    done(tt(S1[:, j0:j0 + nj, :], S1[:, j0:j0 + nj, :], bank[bk][:, 0:nj * P].rearrange("p (j c) -> p j c", j=nj), ADD))
                eng.sem_inc(m_ok, 1)

            eng.wait_ge(gates_ok, 1)
            eng.wait_ge(mt_mm, 1)
            for j in range(RH):
                done(stt(MIX[:, NJ + j, :], bank[j // 2][:, (j % 2) * T:(j % 2 + 1) * T], pcol("gn_w", j), rg[:, j, :], MUL, MUL))
            eng.sem_inc(mt_ok, 1)
            for j in range(NJ):
                done(stt(T4[:, j, :], T4[:, j, :], pcol("ln_b", j), pg[:, j, :], ADD, MUL))
                done(ts(pg[:, j, :], pg[:, j, :], pcol("ln_w", j), None, MUL))
            eng.wait_ge(so_ok, TT)
            nt = lambda g: NTMP.rearrange("p (g c) -> p g c", g=g)
            o64 = pk.rearrange("p a b -> p (a b)").rearrange("p (g c) -> p g c", c=CH)
            head_norm(3, o64, nt(24), 24, CH, stat2, True, 64e-5)
            eng.sem_inc(o_ok, 1)
            og = OG.rearrange("p a b -> p (a b)").rearrange("p (g c) -> p g c", c=P)
            head_norm(4, og, nt(12), 12, P, stat[:, 0:12], False, 1e-6)
            eng.sem_inc(o_ok, 1)
            eng.wait_ge(mt_mm, 2)
            for i in range(3):
                done(tt(MIX[:, 2 * i:2 * i + 2, :].rearrange("p a b -> p (a b)"), bank[4 + i][:],
                        pg[:, 2 * i:2 * i + 2, :].rearrange("p a b -> p (a b)"), MUL))
            done(tt(MIX[:, 0:NJ], MIX[:, 0:NJ], T4, ADD))
            eng.sem_inc(mt_ok, 1)
            eng.wait_ge(mt_mm, 3)
            for j in range(NH):
                bk = (7, 4, 5)[j // 2]
                done(stt(MIX[:, NJ + RH + j, :], bank[bk][:, (j % 2) * T:(j % 2 + 1) * T], pcol("gdn_w", j), gz[:, j, :], MUL, MUL))
            eng.sem_inc(mt_ok, 1)

            eng.wait_ge(x2_in, 16)
            for a in range(TT):
                eng.wait_ge(wo_tile, a + 1)
                for n in range(4):
                    done(tt(X[:, a, n * 512:(n + 1) * 512], X[:, a, n * 512:(n + 1) * 512], bank[a * 4 + n][:], ADD))
            rms(5, X, lambda a: XS[:, a])
            for a in range(TT):
                done(ts(XS[:, a], X[:, a], rstd[:, a:a + 1], None, MUL))
            eng.sem_inc(xs_ok, 1)
            for r in range(8):
                eng.wait_ge(xs_mm, r + 1)
                for kk in range(2):
                    k = 2 * r + kk
                    done(ts(XTT[:, k, :], bank[r % 4][:, kk * T:(kk + 1) * T], pcol("norm2", k), None, MUL))
                eng.sem_inc(xs_t, 1)
            eng.wait_ge(lg_mm, 1)
            for a in range(TT):
                done(tt(LGT[:, a, :], bank[4 + a][:, 0:36], pcol("router_b", 0, 36), ADD))
            gl, el = LGT[:, :, 0:4], LGT[:, :, 4:36]
            s = lambda i: stat[:, 2 * i:2 * i + 2]
            s2 = lambda i: stat2[:, 2 * i:2 * i + 2]
            iota = con("iota")

            def first_max(vals, n, top, tmp, onehot):
                done(v.tensor_reduce(top, vals, AX, MAX))
                done(tt(tmp, vals, wide(top, n), EQ))
                done(ts(tmp, tmp, -99.0, 99.0, MUL, ADD))
                done(tt(tmp, tmp, over(iota[:, 0:n], TT), ADD))
                done(v.tensor_reduce(s2(5), tmp, AX, MIN))
                done(tt(onehot, over(iota[:, 0:n], TT), wide(s2(5), n), EQ))

            first_max(gl, 4, s(0), R6[:, :, 0:4], R3[:, :, 0:4])
            done(tt(R1[:, :, 0:4], gl, wide(s(0), 4), SUB))
            eng.sem_inc(rex_in, 1)
            eng.wait_ge(rex_ok, 1)
            done(v.tensor_reduce(s(1), R2[:, :, 0:4], AX, ADD))
            done(v.reciprocal(s(1), s(1)))
            for a in range(TT):
                done(v.tensor_copy(R4[:, a].rearrange("p (g e) -> p g e", g=4), wide(R3[:, a, 0:4], 8)))
            done(tt(R5, el, R4, MUL))
            done(ts(R4, R4, 1e30, -1e30, MUL, ADD))
            done(tt(R5, R5, R4, ADD))
            first_max(R5, NE, s(2), R6, R3)
            done(stt(R5, R3, -2e30, R5, MUL, ADD))
            first_max(R5, NE, s(3), R6, R4)
            done(tt(s2(0), s(3), s(2), SUB))
            eng.sem_inc(rex_in, 1)
            eng.wait_ge(rex_ok, 2)
            done(ts(s2(1), s2(0), 1.0, None, ADD))
            done(v.reciprocal(s2(1), s2(1)))
            done(tt(s2(1), s2(1), s(1), MUL))
            done(tt(s2(0), s2(0), s2(1), MUL))
            done(tt(R1, R3, R4, ADD))
            eng.sem_inc(e_ok, 1)
            done(tt(R3, R3, wide(s2(1), NE), MUL))
            done(tt(R4, R4, wide(s2(0), NE), MUL))
            done(tt(GE, R3, R4, ADD))
            eng.wait_ge(pos_mm, 1)
            done(stt(posm, bank[6][:, 0:64].rearrange("p (a e) -> p a e", a=TT), 1.0, R1, ADD, MUL))
            done(ts(posm, posm, -1.0, None, ADD))
            done(v.tensor_reduce(s(4)[:, 0:1], bank[6][:, 64:96], AX, MAX))
            done(ts(flag[:], s(4)[:, 0:1], float(TOPC), None, ALU.is_gt))
            eng.sem_inc(flag_ok, 1)

            def gathered(r, quad, c, dst, bk=7):
                eng.wait_ge(g_mm, r * 32 + quad * 4 + (c + 1))
                for kk in range(4):
                    k = 4 * c + kk
                    ts(dst[:, k, :], bank[bk][:, kk * P:(kk + 1) * P], pcol("norm2", k), None, MUL).then_inc(
                        g_ok if kk == 3 else g_part, 1)
                eng.wait_ge(g_part, r * 96 + quad * 12 + (c * 3 + 3))

            def quad_of_experts(r, i, ahead):
                def hid(b):
                    eng.wait_ge(gs_ok, r * NE + i * 4 + (b + 1))
                    if b >= 2:
                        eng.wait_ge(dn_mm, r * NE + i * 4 + (b - 1))
                    tt(HD[b % 2].rearrange("p f s -> p (f s)"), GS, bank[2][:, 64:128], MUL).then_inc(hd_ok, 1)

                cs = slice(i * T, i * T + T) if isinstance(i, int) else bass.ds(i * T, T)
                v.tensor_copy(SGQ, SG.rearrange("p a b -> p (a b)")[:, cs]).then_inc(sgq_ok, 1)
                for b in range(4):
                    hid(b)
                    if ahead:
                        gathered(r, i + 1, b, XN4)
                if ahead:
                    eng.wait_ge(up_mm, r * NE + i * 4 + 4)
                    eng.wait_ge(g_ok, r * 32 + i * 4 + 8)
                    v.tensor_copy(XQ, XN4).then_inc(xq_ok, 1)
                eng.wait_ge(dn_mm, r * NE + i * 4 + 4)
                v.tensor_copy(YS[:, 1024:1536], bank[5][:]).then_inc(yd_half, 1)
                v.tensor_copy(YS[:, 1536:2048], bank[6][:]).then_inc(yd_half, 1)
                eng.wait_ge(yd_half, r * 16 + i * 2 + 2)
                eng.sem_inc(yd_ok, 1)
                for q in range(8):
                    a, n = q // 4, q % 4
                    eng.wait_ge(sc_mm, (r * 8 + i) * 8 + (q + 1))
                    c = slice(n * 512, (n + 1) * 512)
                    tt(X[:, a, c], X[:, a, c], bank[7 if q % 2 else 2][:], ADD).then_inc(sc_ok, 1)
                eng.wait_ge(sc_ok, (r * 8 + i) * 8 + 8)

            def experts(r):
                sl = lambda t, a: t[:, a].rearrange("p (e s) -> p e s", e=NE)
                for n, es in enumerate((slice(0, 4), slice(4, NE))):
                    for a in range(TT):
                        one(tt(sl(PS, a)[:, es], over(iota, es.stop - es.start), wide(posm[:, a, es], TOPC), EQ), r, 2 * n + a)
                    if n == 0:
                        eng.sem_inc(p_ok, 1)
                for a in range(TT):
                    one(tt(sl(PG, a), sl(PS, a), wide(GE[:, a], TOPC), MUL), r, 4 + a)
                eng.sem_inc(pg_ok, 1)
                one(ts(posm, posm, -float(TOPC), None, ADD), r, 6)
                for c in range(4):
                    gathered(r, 0, c, XQ, 3 + c)
                eng.wait_ge(g_ok, r * 32 + 4)
                eng.wait_ge(sg_ok, r * 4 + 4)
                eng.sem_inc(xq_ok, 1)
                with eng.Fori(0, 7) as i:
                    quad_of_experts(r, i, True)
                quad_of_experts(r, 7, False)

            def one(ins, r, n):
                ins.then_inc(p_step, 1)
                eng.wait_ge(p_step, r * 7 + (n + 1))

            experts(0)
            with eng.If(eng.value_load(flag[0:1, 0:1]) == 1):
                with eng.Fori(1, PASSES) as r:
                    experts(r)
            rms(6, X, lambda a: JUNK)
            eng.wait_ge(fw_in, 16)
            for a in range(TT):
                stt(X[:, a], X[:, a], rstd[:, a:a + 1], FW, MUL, MUL).then_inc(y_ok, 1)


class Steps:

    def __init__(self, eng, sem):
        self.eng, self.sem, self.n = eng, sem, 0

    def __call__(self, ins):
        self.n += 1
        ins.then_inc(self.sem, 1)
        self.eng.wait_ge(self.sem, self.n)


def kernel(**inputs):
    import concourse.bacc as bacc
    from concourse.bass_utils import run_bass_kernel_spmd

    a = {n: np.ascontiguousarray(v) for n, v in inputs.items()}

    def rows(v):
        return v.reshape(-1, P).T

    def alike(v):
        return np.broadcast_to(v.reshape(1, -1), (P, v.size))

    par = np.concatenate([rows(a["rwkv_mu_rkvg"]), rows(a["rwkv_w0"]), rows(a["rwkv_a0"]), rows(a["rwkv_k_k"]), rows(a["rwkv_k_a"]),
                          rows(a["rwkv_r_k"]), rows(a["rwkv_ln_w"]), rows(a["rwkv_ln_b"]), rows(a["ret_gn_w"]), rows(a["gdn_norm_w"]),
                          rows(a["gdn_conv_w"]), a["norm1_w"].reshape(P, K), a["rwkv_mu_wa"][0, 0].reshape(P, K),
                          a["rwkv_mu_wa"][0, 1].reshape(P, K), a["norm2_w"].reshape(P, K), alike(a["gdn_dt_bias"]),
                          alike(a["gdn_a_log"]), alike(a["moe_group_b"]), alike(a["moe_expert_b"])], axis=1)
    feeds = {
        "x": a["x"].reshape(T, D),
        "positions": np.ascontiguousarray(a["positions"].reshape(TT, P).T),
        "w_in": a["w_in"].reshape(D, N_IN),
        "w_out": a["w_out"].reshape(D, D),
        "lora1": np.stack([a["rwkv_w1"][0], a["rwkv_a1"][0]]),
        "lora2": np.stack([a["rwkv_w2"][0], a["rwkv_a2"][0]], axis=1),
        "par": np.ascontiguousarray(par),
        "consts": np.concatenate(list(const_arrays().values()), axis=1),
        "router": np.concatenate([a["moe_group_w"][0], a["moe_expert_w"][0]], axis=1),
        "w1": a["moe_w1"].reshape(NE, D, HID),
        "w3": a["moe_w3"].reshape(NE, D, HID),
        "w2": a["moe_w2"].reshape(NE, HID, D),
        "final_w": np.ascontiguousarray(alike(a["final_norm_w"])),
    }
    nc = bacc.Bacc("TRN2", target_bir_lowering=False, num_devices=1)
    aps = [nc.dram_tensor(n, v.shape, mybir.dt.from_np(v.dtype), kind="ExternalInput").ap() for n, v in feeds.items()]
    out = nc.dram_tensor("out", (T, D), F32, kind="ExternalOutput").ap()
    trunk(nc, *aps, out)
    return run_bass_kernel_spmd(nc, [feeds], core_ids=[0]).results[0]["out"].reshape(1, T, D)
```
